# Optimizing a Trainium2 kernel written in Bass

```python
import jax, jax.numpy as jnp
from jax import lax
import numpy as np
import math

D_MODEL = 1024
BATCH = 1
SEQ = 512
DEPTH = 1

HEAD_DIM = 64
ROPE_THETA = 10000.0
NORM_EPS = 1e-6
NEG = -1e30
NSA_HEADS = 12
NSA_KV_GROUPS = 3
NSA_HPG = NSA_HEADS // NSA_KV_GROUPS
CMP_BLOCK = 32
CMP_STRIDE = 16
CMP_HIDDEN = 256
SLC_BLOCK = 64
SLC_TOPK = 16
WIN_SIZE = 512
SLC_Q_BLOCK = 64
WIN_Q_BLOCK = 128
DIL_PAIRS = ((128, 1), (512, 4), (2048, 16))
DIL_GROUPS = len(DIL_PAIRS)
DIL_HPG = 4
DIL_HEADS = DIL_GROUPS * DIL_HPG
DIL_NKEYS = max(w // d + 1 for w, d in DIL_PAIRS)
DIL_Q_BLOCK = 128
D_FF = 4 * D_MODEL
Q_A_COLS = NSA_HEADS * HEAD_DIM
KV_A_COLS = NSA_KV_GROUPS * HEAD_DIM
GATE_A_COLS = 3 * NSA_HEADS
QKV_B_COLS = DIL_HEADS * HEAD_DIM
IN_SIZES = (Q_A_COLS, KV_A_COLS, KV_A_COLS, KV_A_COLS, KV_A_COLS, KV_A_COLS, KV_A_COLS,
            GATE_A_COLS, QKV_B_COLS, QKV_B_COLS, QKV_B_COLS, D_MODEL, D_MODEL)
IN_COLS = sum(IN_SIZES)
SPLIT_POINTS = tuple(int(c) for c in np.cumsum(IN_SIZES)[:-1])


def _rmsnorm(x, g):
    xf = x.astype(jnp.float32)
    y = xf * lax.rsqrt(jnp.mean(xf * xf, axis=-1, keepdims=True) + NORM_EPS)
    return (y * g.astype(jnp.float32)).astype(x.dtype)

def _rope(x, pos):
    half = HEAD_DIM // 2
    inv_freq = jnp.power(ROPE_THETA, -jnp.arange(half, dtype=jnp.float32) / half)
    ang = jnp.asarray(pos, jnp.float32)[:, None] * inv_freq[None, :]
    shape = (1, ang.shape[0]) + (1,) * (x.ndim - 3) + (half,)
    cos = jnp.cos(ang).reshape(shape)
    sin = jnp.sin(ang).reshape(shape)
    xf = x.astype(jnp.float32)
    x1, x2 = xf[..., :half], xf[..., half:]
    return jnp.concatenate([x1 * cos - x2 * sin, x2 * cos + x1 * sin], axis=-1).astype(x.dtype)

def _masked_softmax(s, mask):
    s = jnp.where(mask, s.astype(jnp.float32), NEG)
    return jax.nn.softmax(s, axis=-1) * mask

def _compress(kv, pos_emb, w1, w2):
    B, S, G, dh = kv.shape
    n_cmp = (S - CMP_BLOCK) // CMP_STRIDE + 1
    idx = np.arange(n_cmp)[:, None] * CMP_STRIDE + np.arange(CMP_BLOCK)[None, :]
    blocks = kv[:, idx] + pos_emb[None, None, :, None, :]
    blocks = jnp.transpose(blocks, (0, 1, 3, 2, 4)).reshape(B, n_cmp, G, CMP_BLOCK * dh)
    return jax.nn.gelu(blocks @ w1) @ w2

def _cmp_to_slc_overlap(n_cmp, n_slc):
    cs = np.arange(n_cmp)[:, None] * CMP_STRIDE
    ss = np.arange(n_slc)[None, :] * SLC_BLOCK
    ov = np.minimum(cs + CMP_BLOCK, ss + SLC_BLOCK) - np.maximum(cs, ss)
    return (np.clip(ov, 0, None) / CMP_BLOCK).astype(np.float32)

def _nsa_mixer(q, k_cmp, v_cmp, k_slc, v_slc, k_win, v_win, gate,
               k_norm_cmp, cmp_k_pos, cmp_k_w1, cmp_k_w2, cmp_v_pos, cmp_v_w1, cmp_v_w2):
    B, S = q.shape[0], q.shape[1]
    G, R, dh = NSA_KV_GROUPS, NSA_HPG, HEAD_DIM
    scale = dh ** -0.5
    t = np.arange(S)

    kc = _compress(k_cmp, cmp_k_pos, cmp_k_w1, cmp_k_w2)
    vc = _compress(v_cmp, cmp_v_pos, cmp_v_w1, cmp_v_w2)
    n_cmp = kc.shape[1]
    c_end = np.arange(n_cmp) * CMP_STRIDE + CMP_BLOCK - 1
    kc = _rope(_rmsnorm(kc, k_norm_cmp), c_end)
    s_cmp = jnp.einsum("bsgrd,bcgd->bgrsc", q, kc) * scale
    p_cmp = _masked_softmax(s_cmp, c_end[None, :] <= t[:, None])
    o_cmp = jnp.einsum("bgrsc,bcgd->bsgrd", p_cmp.astype(vc.dtype), vc)

    n_slc = S // SLC_BLOCK
    top_n = min(SLC_TOPK, n_slc)
    overlap = jnp.asarray(_cmp_to_slc_overlap(n_cmp, n_slc))
    imp = jnp.einsum("bgrsc,cn->bgsn", p_cmp, overlap)
    blk = np.arange(n_slc)[None, :]
    cur = (t // SLC_BLOCK)[:, None]
    forced = (blk == 0) | (blk == cur) | (blk == cur - 1)
    score = jnp.where(forced, jnp.inf, jnp.where(blk <= cur, imp, -jnp.inf))
    top_score, top_idx = lax.top_k(score, top_n)
    top_ok = top_score > -jnp.inf

    kb = jnp.transpose(k_slc.reshape(B, n_slc, SLC_BLOCK, G, dh), (0, 3, 1, 2, 4))
    vb = jnp.transpose(v_slc.reshape(B, n_slc, SLC_BLOCK, G, dh), (0, 3, 1, 2, 4))
    gather_blocks = jax.vmap(jax.vmap(lambda kk, ii: kk[ii]))
    nqs = S // SLC_Q_BLOCK

    def slc_block(xs):
        qc, idx, ok, tq = xs
        ks = gather_blocks(kb, idx)
        vs = gather_blocks(vb, idx)
        s = jnp.einsum("bqgrd,bgqnkd->bgrqnk", qc, ks) * scale
        kpos = idx[..., None] * SLC_BLOCK + np.arange(SLC_BLOCK)
        mask = ok[..., None] & (kpos <= tq[:, None, None])
        s = s.reshape(B, G, R, SLC_Q_BLOCK, top_n * SLC_BLOCK)
        mask = mask.reshape(B, G, 1, SLC_Q_BLOCK, top_n * SLC_BLOCK)
        p = _masked_softmax(s, mask)
        vs = vs.reshape(B, G, SLC_Q_BLOCK, top_n * SLC_BLOCK, dh)
        return jnp.einsum("bgrqj,bgqjd->bqgrd", p.astype(vs.dtype), vs)

    qs = jnp.moveaxis(q.reshape(B, nqs, SLC_Q_BLOCK, G, R, dh), 1, 0)
    idx_s = jnp.moveaxis(top_idx.reshape(B, G, nqs, SLC_Q_BLOCK, top_n), 2, 0)
    ok_s = jnp.moveaxis(top_ok.reshape(B, G, nqs, SLC_Q_BLOCK, top_n), 2, 0)
    tq_s = jnp.arange(S, dtype=jnp.int32).reshape(nqs, SLC_Q_BLOCK)
    o_slc = lax.map(slc_block, (qs, idx_s, ok_s, tq_s))
    o_slc = jnp.moveaxis(o_slc, 0, 1).reshape(B, S, G, R, dh)

    span = WIN_SIZE + WIN_Q_BLOCK
    kw_pad = jnp.pad(k_win, ((0, 0), (WIN_SIZE, 0), (0, 0), (0, 0)))
    vw_pad = jnp.pad(v_win, ((0, 0), (WIN_SIZE, 0), (0, 0), (0, 0)))
    nqw = S // WIN_Q_BLOCK

    def win_block(xs):
        qc, start = xs
        ks = lax.dynamic_slice_in_dim(kw_pad, start, span, axis=1)
        vs = lax.dynamic_slice_in_dim(vw_pad, start, span, axis=1)
        s = jnp.einsum("bqgrd,bkgd->bgrqk", qc, ks) * scale
        tq = start + jnp.arange(WIN_Q_BLOCK)
        kp = start - WIN_SIZE + jnp.arange(span)
        diff = tq[:, None] - kp[None, :]
        mask = (diff >= 0) & (diff < WIN_SIZE) & (kp[None, :] >= 0)
        p = _masked_softmax(s, mask)
        return jnp.einsum("bgrqk,bkgd->bqgrd", p.astype(vs.dtype), vs)

    qw = jnp.moveaxis(q.reshape(B, nqw, WIN_Q_BLOCK, G, R, dh), 1, 0)
    starts = jnp.arange(nqw, dtype=jnp.int32) * WIN_Q_BLOCK
    o_win = lax.map(win_block, (qw, starts))
    o_win = jnp.moveaxis(o_win, 0, 1).reshape(B, S, G, R, dh)

    y = gate[..., 0:1] * o_cmp + gate[..., 1:2] * o_slc + gate[..., 2:3] * o_win
    return y.reshape(B, S, G * R * dh)

def _dilated_mixer(q, k, v):
    B, S = q.shape[0], q.shape[1]
    dh = HEAD_DIM
    scale = dh ** -0.5
    dil = np.array([d for _, d in DIL_PAIRS])
    win = np.array([w for w, _ in DIL_PAIRS])
    j = np.arange(DIL_NKEYS)
    in_window = (j[None, :] * dil[:, None]) <= win[:, None]
    kg = jnp.transpose(k, (2, 0, 1, 3, 4))
    vg = jnp.transpose(v, (2, 0, 1, 3, 4))
    gather_stride = jax.vmap(lambda kk, ii: kk[:, ii])
    nq = S // DIL_Q_BLOCK

    def dil_block(xs):
        qc, tq = xs
        kpos = tq[None, :, None] - j[None, None, :] * dil[:, None, None]
        mask = (kpos >= 0) & in_window[:, None, :]
        idx = jnp.maximum(kpos, 0)
        ks = gather_stride(kg, idx)
        vs = gather_stride(vg, idx)
        s = jnp.einsum("gbqhd,gbqjhd->gbhqj", qc, ks).astype(jnp.float32) * scale
        s = jnp.where(mask[:, None, None], s, NEG)
        m = jnp.max(s, axis=-1, keepdims=True)
        e = jnp.exp(s - m)
        den = jnp.sum(e, axis=-1, keepdims=True)
        o = jnp.einsum("gbhqj,gbqjhd->gbqhd", (e / den).astype(vs.dtype), vs)
        lse = (m + jnp.log(den))[..., 0]
        w = jax.nn.softmax(lse, axis=0)
        return jnp.einsum("gbhq,gbqhd->bqhd", w.astype(o.dtype), o)

    qd = jnp.moveaxis(jnp.transpose(q, (2, 0, 1, 3, 4)).reshape(DIL_GROUPS, B, nq, DIL_Q_BLOCK, DIL_HPG, dh), 2, 0)
    tq_d = jnp.arange(S, dtype=jnp.int32).reshape(nq, DIL_Q_BLOCK)
    o = lax.map(dil_block, (qd, tq_d))
    return jnp.moveaxis(o, 0, 1).reshape(B, S, DIL_HPG * dh)

def first_inputs(seed: int = 0) -> dict:
    key = jax.random.key(seed)
    ks = jax.random.split(key, 21)
    L = DEPTH

    def nrm(k, shape, scale):
        return scale * jax.random.normal(k, shape, jnp.float32)

    def gain(k, n):
        return 1.0 + 0.02 * jax.random.normal(k, (L, n), jnp.float32)

    return {
        "x": jax.random.normal(ks[0], (BATCH, SEQ, D_MODEL), jnp.float32),
        "norm1_g": gain(ks[1], D_MODEL),
        "w_in": nrm(ks[2], (L, D_MODEL, IN_COLS), D_MODEL ** -0.5),
        "q_norm_a": gain(ks[3], HEAD_DIM),
        "k_norm_cmp": gain(ks[4], HEAD_DIM),
        "k_norm_slc": gain(ks[5], HEAD_DIM),
        "k_norm_win": gain(ks[6], HEAD_DIM),
        "cmp_k_pos": nrm(ks[7], (L, CMP_BLOCK, HEAD_DIM), 0.2),
        "cmp_k_w1": nrm(ks[8], (L, CMP_BLOCK * HEAD_DIM, CMP_HIDDEN), (CMP_BLOCK * HEAD_DIM) ** -0.5),
        "cmp_k_w2": nrm(ks[9], (L, CMP_HIDDEN, HEAD_DIM), CMP_HIDDEN ** -0.5),
        "cmp_v_pos": nrm(ks[10], (L, CMP_BLOCK, HEAD_DIM), 0.2),
        "cmp_v_w1": nrm(ks[11], (L, CMP_BLOCK * HEAD_DIM, CMP_HIDDEN), (CMP_BLOCK * HEAD_DIM) ** -0.5),
        "cmp_v_w2": nrm(ks[12], (L, CMP_HIDDEN, HEAD_DIM), CMP_HIDDEN ** -0.5),
        "q_norm_b": gain(ks[13], HEAD_DIM),
        "k_norm_b": gain(ks[14], HEAD_DIM),
        "w_o_a": nrm(ks[15], (L, Q_A_COLS, D_MODEL), Q_A_COLS ** -0.5),
        "w_o_b": nrm(ks[16], (L, DIL_HPG * HEAD_DIM, D_MODEL), (DIL_HPG * HEAD_DIM) ** -0.5),
        "w_out": nrm(ks[17], (L, D_MODEL, D_MODEL), D_MODEL ** -0.5),
        "norm2_g": gain(ks[18], D_MODEL),
        "w_up": nrm(ks[19], (L, D_MODEL, D_FF), D_MODEL ** -0.5),
        "w_down": nrm(ks[20], (L, D_FF, D_MODEL), D_FF ** -0.5),
    }

def first_block(x, norm1_g, w_in, q_norm_a, k_norm_cmp, k_norm_slc, k_norm_win,
              cmp_k_pos, cmp_k_w1, cmp_k_w2, cmp_v_pos, cmp_v_w1, cmp_v_w2,
              q_norm_b, k_norm_b, w_o_a, w_o_b, w_out, norm2_g, w_up, w_down):
    B, S = x.shape[0], x.shape[1]
    G, R, dh = NSA_KV_GROUPS, NSA_HPG, HEAD_DIM
    pos = np.arange(S)
    for i in range(DEPTH):
        h = _rmsnorm(x, norm1_g[i])
        proj = h @ w_in[i]
        (q_a, k_c, v_c, k_s, v_s, k_w, v_w, g_nsa,
         q_b, k_b, v_b, g_ma, g_mb) = jnp.split(proj, SPLIT_POINTS, axis=-1)

        q_a = _rope(_rmsnorm(q_a.reshape(B, S, NSA_HEADS, dh), q_norm_a[i]), pos).reshape(B, S, G, R, dh)
        k_c = k_c.reshape(B, S, G, dh)
        v_c = v_c.reshape(B, S, G, dh)
        k_s = _rope(_rmsnorm(k_s.reshape(B, S, G, dh), k_norm_slc[i]), pos)
        v_s = v_s.reshape(B, S, G, dh)
        k_w = _rope(_rmsnorm(k_w.reshape(B, S, G, dh), k_norm_win[i]), pos)
        v_w = v_w.reshape(B, S, G, dh)
        g_nsa = jax.nn.sigmoid(g_nsa).reshape(B, S, G, R, 3)
        y_a = _nsa_mixer(q_a, k_c, v_c, k_s, v_s, k_w, v_w, g_nsa,
                         k_norm_cmp[i], cmp_k_pos[i], cmp_k_w1[i], cmp_k_w2[i],
                         cmp_v_pos[i], cmp_v_w1[i], cmp_v_w2[i])

        q_b = _rope(_rmsnorm(q_b.reshape(B, S, DIL_HEADS, dh), q_norm_b[i]), pos)
        k_b = _rope(_rmsnorm(k_b.reshape(B, S, DIL_HEADS, dh), k_norm_b[i]), pos)
        y_b = _dilated_mixer(q_b.reshape(B, S, DIL_GROUPS, DIL_HPG, dh),
                             k_b.reshape(B, S, DIL_GROUPS, DIL_HPG, dh),
                             v_b.reshape(B, S, DIL_GROUPS, DIL_HPG, dh))

        mixed = jax.nn.sigmoid(g_ma) * (y_a @ w_o_a[i]) + jax.nn.sigmoid(g_mb) * (y_b @ w_o_b[i])
        x = x + mixed @ w_out[i]

        h2 = _rmsnorm(x, norm2_g[i])
        x = x + jnp.square(jax.nn.relu(h2 @ w_up[i])) @ w_down[i]
    return x


DEPTH_2 = 2

DIFF_HEADS = 4
DIFF_HEAD_DIM = 64
DIFF_WIDTH = DIFF_HEADS * 2 * DIFF_HEAD_DIM
SB_HEADS = 8
SB_HEAD_DIM = 64
SB_WIDTH = SB_HEADS * SB_HEAD_DIM
IN_COLS_2 = 3 * DIFF_WIDTH + 3 * SB_WIDTH + 2 * D_MODEL
FFN_HIDDEN = -(-(8 * D_MODEL) // (3 * 256)) * 256
Q_BLOCK = 128


def rms_norm(x, g):
    xf = x.astype(jnp.float32)
    y = xf * lax.rsqrt(jnp.mean(xf * xf, axis=-1, keepdims=True) + NORM_EPS)
    return (y * g.astype(jnp.float32)).astype(x.dtype)

def rope_tables(seq, dim):
    pos = jnp.arange(seq, dtype=jnp.float32)
    inv = ROPE_THETA ** (-jnp.arange(0, dim, 2, dtype=jnp.float32) / dim)
    ang = pos[:, None] * inv[None, :]
    return jnp.cos(ang), jnp.sin(ang)

def apply_rope(t, cos, sin):
    c = cos[None, :, None, :].astype(t.dtype)
    s = sin[None, :, None, :].astype(t.dtype)
    t1, t2 = jnp.split(t, 2, axis=-1)
    return jnp.concatenate([t1 * c - t2 * s, t2 * c + t1 * s], axis=-1)

def to_blocks(t):
    b, h, s, d = t.shape
    return t.reshape(b, h, s // Q_BLOCK, Q_BLOCK, d).transpose(2, 0, 1, 3, 4)

def from_blocks(o):
    nb, b, h, q, dv = o.shape
    return o.transpose(1, 0, 3, 2, 4).reshape(b, nb * q, h, dv)

def diff_attention(q1, q2, k1, k2, v, lam):
    s_len = k1.shape[2]
    kpos = jnp.arange(s_len)
    qpos_blocks = kpos.reshape(-1, Q_BLOCK)
    scale = DIFF_HEAD_DIM ** -0.5

    def block(args):
        qb1, qb2, qpos = args
        mask = kpos[None, :] <= qpos[:, None]

        def probs(qb, k):
            sc = jnp.einsum('bhqd,bhkd->bhqk', qb, k).astype(jnp.float32) * scale
            sc = jnp.where(mask, sc, -jnp.inf)
            return jax.nn.softmax(sc, axis=-1)

        w = probs(qb1, k1) - lam * probs(qb2, k2)
        return jnp.einsum('bhqk,bhkd->bhqd', w.astype(v.dtype), v)

    o = lax.map(block, (to_blocks(q1), to_blocks(q2), qpos_blocks))
    return from_blocks(o)

def stick_breaking_attention(q, k, v):
    s_len = k.shape[2]
    kpos = jnp.arange(s_len)
    qpos_blocks = kpos.reshape(-1, Q_BLOCK)
    scale = SB_HEAD_DIM ** -0.5

    def block(args):
        qb, qpos = args
        mask = kpos[None, :] < qpos[:, None]
        z = jnp.einsum('bhqd,bhkd->bhqk', qb, k).astype(jnp.float32) * scale
        log_beta = jax.nn.log_sigmoid(z)
        log_rem = jnp.where(mask, jax.nn.log_sigmoid(-z), 0.0)
        key_axis = log_rem.ndim - 1
        after = lax.cumsum(log_rem, axis=key_axis, reverse=True) - log_rem
        a = jnp.where(mask, jnp.exp(log_beta + after), 0.0)
        return jnp.einsum('bhqk,bhkd->bhqd', a.astype(v.dtype), v)

    o = lax.map(block, (to_blocks(q), qpos_blocks))
    return from_blocks(o)

def hybrid_layer(x, cos, sin, layer, g_attn, w_in, b_gate, lam_p, subln, w_o_diff, w_o_sb,
                 w_out, g_ffn, w_ffn_in, w_ffn_out):
    b, s, _ = x.shape
    h = rms_norm(x, g_attn)
    proj = h @ w_in
    offs = np.cumsum([DIFF_WIDTH, DIFF_WIDTH, DIFF_WIDTH, SB_WIDTH, SB_WIDTH, SB_WIDTH]).tolist()
    dq, dk, dv, sq, sk, sv, gates = jnp.split(proj, offs, axis=-1)

    dq = apply_rope(dq.reshape(b, s, 2 * DIFF_HEADS, DIFF_HEAD_DIM), cos, sin)
    dk = apply_rope(dk.reshape(b, s, 2 * DIFF_HEADS, DIFF_HEAD_DIM), cos, sin)
    dq = dq.reshape(b, s, DIFF_HEADS, 2, DIFF_HEAD_DIM).transpose(3, 0, 2, 1, 4)
    dk = dk.reshape(b, s, DIFF_HEADS, 2, DIFF_HEAD_DIM).transpose(3, 0, 2, 1, 4)
    dv = dv.reshape(b, s, DIFF_HEADS, 2 * DIFF_HEAD_DIM).transpose(0, 2, 1, 3)
    lam_init = 0.8 - 0.6 * math.exp(-0.3 * layer)
    lp = lam_p.astype(jnp.float32)
    lam = jnp.exp(jnp.sum(lp[0] * lp[1])) - jnp.exp(jnp.sum(lp[2] * lp[3])) + lam_init
    o_diff = diff_attention(dq[0], dq[1], dk[0], dk[1], dv, lam)
    o_diff = (rms_norm(o_diff, subln) * (1.0 - lam_init)).reshape(b, s, DIFF_WIDTH)

    sq = sq.reshape(b, s, SB_HEADS, SB_HEAD_DIM).transpose(0, 2, 1, 3)
    sk = sk.reshape(b, s, SB_HEADS, SB_HEAD_DIM).transpose(0, 2, 1, 3)
    sv = sv.reshape(b, s, SB_HEADS, SB_HEAD_DIM).transpose(0, 2, 1, 3)
    o_sb = stick_breaking_attention(sq, sk, sv).reshape(b, s, SB_WIDTH)

    g_diff, g_sb = jnp.split(jax.nn.sigmoid(gates + b_gate), 2, axis=-1)
    merged = g_diff * (o_diff @ w_o_diff) + g_sb * (o_sb @ w_o_sb)
    x = x + merged @ w_out

    h2 = rms_norm(x, g_ffn)
    gate, up = jnp.split(h2 @ w_ffn_in, 2, axis=-1)
    return x + (jax.nn.silu(gate) * up) @ w_ffn_out

def second_inputs(seed: int = 0) -> dict:
    key = jax.random.key(seed)
    ks = jax.random.split(key, 14)
    f32 = jnp.float32
    nrm = lambda k, shape, scale: jax.random.normal(k, shape, f32) * scale
    return {
        "x": nrm(ks[0], (BATCH, SEQ, D_MODEL), 1.0),
        "norm_attn": 1.0 + nrm(ks[1], (DEPTH_2, D_MODEL), 0.02),
        "w_in": nrm(ks[2], (DEPTH_2, D_MODEL, IN_COLS_2), D_MODEL ** -0.5),
        "b_gate": nrm(ks[3], (DEPTH_2, 2 * D_MODEL), 0.02),
        "diff_lambda": nrm(ks[4], (DEPTH_2, 4, DIFF_HEAD_DIM), 0.1),
        "diff_subln": 1.0 + nrm(ks[5], (DEPTH_2, 2 * DIFF_HEAD_DIM), 0.02),
        "w_o_diff": nrm(ks[6], (DEPTH_2, DIFF_WIDTH, D_MODEL), DIFF_WIDTH ** -0.5),
        "w_o_sb": nrm(ks[7], (DEPTH_2, SB_WIDTH, D_MODEL), SB_WIDTH ** -0.5),
        "w_out": nrm(ks[8], (DEPTH_2, D_MODEL, D_MODEL), D_MODEL ** -0.5),
        "norm_ffn": 1.0 + nrm(ks[9], (DEPTH_2, D_MODEL), 0.02),
        "w_ffn_in": nrm(ks[10], (DEPTH_2, D_MODEL, 2 * FFN_HIDDEN), D_MODEL ** -0.5),
        "w_ffn_out": nrm(ks[11], (DEPTH_2, FFN_HIDDEN, D_MODEL), FFN_HIDDEN ** -0.5),
        "norm_final": 1.0 + nrm(ks[12], (D_MODEL,), 0.02),
    }

def second_block(x, norm_attn, w_in, b_gate, diff_lambda, diff_subln, w_o_diff, w_o_sb, w_out,
              norm_ffn, w_ffn_in, w_ffn_out, norm_final):
    cos, sin = rope_tables(x.shape[1], DIFF_HEAD_DIM)
    for layer in range(DEPTH_2):
        x = hybrid_layer(x, cos, sin, layer, norm_attn[layer], w_in[layer], b_gate[layer],
                         diff_lambda[layer], diff_subln[layer], w_o_diff[layer], w_o_sb[layer],
                         w_out[layer], norm_ffn[layer], w_ffn_in[layer], w_ffn_out[layer])
    return rms_norm(x, norm_final)


def setup_inputs(seed=0):
    out = dict(first_inputs(seed))
    for name, value in second_inputs(seed + 1).items():
        if name != "x":
            out[name + "_2"] = value
    return out


def reference(
    x, norm1_g, w_in, q_norm_a, k_norm_cmp, k_norm_slc, k_norm_win, cmp_k_pos, cmp_k_w1,
    cmp_k_w2, cmp_v_pos, cmp_v_w1, cmp_v_w2, q_norm_b, k_norm_b, w_o_a, w_o_b, w_out, norm2_g,
    w_up, w_down, norm_attn_2, w_in_2, b_gate_2, diff_lambda_2, diff_subln_2, w_o_diff_2,
    w_o_sb_2, w_out_2, norm_ffn_2, w_ffn_in_2, w_ffn_out_2, norm_final_2,
):
    x = first_block(
        x, norm1_g, w_in, q_norm_a, k_norm_cmp, k_norm_slc, k_norm_win, cmp_k_pos, cmp_k_w1,
        cmp_k_w2, cmp_v_pos, cmp_v_w1, cmp_v_w2, q_norm_b, k_norm_b, w_o_a, w_o_b, w_out,
        norm2_g, w_up, w_down,
    )
    return second_block(
        x, norm_attn_2, w_in_2, b_gate_2, diff_lambda_2, diff_subln_2, w_o_diff_2, w_o_sb_2,
        w_out_2, norm_ffn_2, w_ffn_in_2, w_ffn_out_2, norm_final_2,
    )


_drawn_inputs = setup_inputs


def setup_inputs(seed=0):
    import zlib

    import numpy as np

    out = dict(_drawn_inputs(seed))
    spreads = {}
    factors = {'norm1_g': 8.0,
     'q_norm_a': 8.0,
     'k_norm_cmp': 8.0,
     'k_norm_slc': 8.0,
     'k_norm_win': 8.0,
     'cmp_k_pos': 4.713,
     'q_norm_b': 8.0,
     'k_norm_b': 8.0,
     'norm2_g': 2.931,
     'norm_attn_2': 4.731,
     'b_gate_2': 8.0,
     'diff_lambda_2': 5.814,
     'diff_subln_2': 29.142,
     'norm_ffn_2': 4.293,
     'norm_final_2': 7.961}
    for name, (base, spread) in spreads.items():
        noise = np.random.default_rng([zlib.crc32(name.encode()), seed]).standard_normal(out[name].shape)
        drawn = base * np.exp(spread * noise) if base else spread * noise
        out[name] = __import__('jax').numpy.asarray(drawn.astype(out[name].dtype))
    for name, factor in factors.items():
        out[name] = (out[name] * factor).astype(out[name].dtype)
    return out
```

```python
from contextlib import ExitStack

import concourse.bass as bass
from concourse import mybir

F32 = mybir.dt.float32
F32R = mybir.dt.float32r
BF16 = mybir.dt.bfloat16
ALU = mybir.AluOpType
ACT = mybir.ActivationFunctionType
AX_X = mybir.AxisListType.X

P = 128
S = 512
D = 1024
QT = S // P
KT = D // P
HD = 64
HALF = HD // 2
EPS = 1e-6
BANK = 512
NEG = -1e30
FF1 = 4 * D
FF2 = 2816
LAYERS = 2
NSA_HEADS, NSA_GROUPS = 12, 3
CMP_N, CMP_PAD, CMP_STRIDE, CMP_LEN = 31, 32, 16, 32
CMP_HID = 256
DIL_GROUPS, DIL_HPG = 3, 4
BLK = 4
RAW_RING, SPLIT_RING = 2, 3
BLK_COLS = BLK * BANK
GELU_A, GELU_B = 0.044715, 1.5957691216057308

CAUSAL, BAND, MOD4, MOD4C, MOD16, MOD16C, STRICT = range(7)
N_MASK = 7
(G_QA, G_KC, G_KS, G_KW, G_QB, G_KB) = range(6)

C_COS, C_SIN, C_COSC, C_SINC, C_VALID, C_ID = 0, 256, 512, 576, 640, 641
C_ALL = C_ID + P
M_ALL = N_MASK * P + QT * CMP_PAD


class Block:

    def __init__(self, pieces, split=True):
        self.pieces, self.split = pieces, split
        self.kts = max(p[5] + p[2] for p in pieces)
        self.width = max(p[6] + p[4] for p in pieces)


class Panel:

    def __init__(self, blocks, width, kts=None, rope=None, turn=False, twice=False, query=False, dest=None, tile0=0,
                 col=0, src=None, up=False, group=0, tiles=0, split_at=None):
        self.blocks, self.width, self.kts = blocks, width, kts
        self.rope, self.turn, self.twice, self.query = rope, turn, twice, query
        self.dest, self.tile0, self.col, self.src = dest, tile0, col, src
        self.up, self.group, self.tiles, self.split_at = up, group, tiles, split_at


def panel(pieces, kts=KT, row=0, **what):
    blocks, k = [], 0
    while k < kts:
        n = min(BLK, kts - k)
        at, ps = 0, []
        for m, c, w in pieces:
            ps.append((m, row + k * P, n, c, w, 0, at))
            at += w
        blocks.append(Block(ps))
        k += n
    return Panel(blocks, at, kts=kts, **what)


def make_plan():
    w = "w_in"
    qa, kc, ks, vs, kw, vw, gn = 0, 768, 1152, 1344, 1536, 1728, 1920
    qb, kb, vb, gm = 1956, 2724, 3492, 4260
    first = [
        ("norm", [], dict(gain="norm1")),
        ("proj", [
            panel([(w, qa, 512)], rope=G_QA, dest="qa", tile0=0, query=True),
            panel([(w, qa + 512, 256)], rope=G_QA, dest="qa", tile0=4, query=True),
            panel([(w, ks, 192)], rope=G_KS, dest="ks", tile0=0, twice=True),
            panel([(w, kw, 192)], rope=G_KW, dest="kw", tile0=0, twice=True),
            panel([(w, kc, 192)], turn=True, dest="cmp_in", tile0=0, twice=True),
            panel([(w, kc + 192, 192)], turn=True, dest="cmp_in", tile0=3, twice=True),
            panel([(w, vs, 192), (w, vw, 192), (w, gn, 36)], dest="nsa_v")], dict(who="nsa")),
        ("compress", [Panel([Block([(m, k * 8 * P, 8, 0, CMP_HID, 0, 0)], split=False)
                             for m in ("cmp_k_w1", "cmp_v_w1") for k in range(2)], CMP_HID)], {}),
        ("attend", [], dict(who="nsa")),
        ("turn", [], dict(src="y_nsa", tiles=6, tile0=0)),
        ("proj", [
            *[panel([(w, qb + 256 * n, 256)], rope=G_QB, dest="qb", tile0=2 * n, query=True) for n in range(3)],
            *[panel([(w, kb + 256 * n, 256)], rope=G_KB, dest="kb", tile0=2 * n) for n in range(3)],
            panel([(w, vb, 512)], dest="vb", col=0),
            panel([(w, vb + 512, 256)], dest="vb", col=512)], dict(who="dil")),
        ("attend", [], dict(who="dil")),
        ("turn", [], dict(src="y_dil", tiles=2, tile0=6)),
        ("gates", [panel([(w, gm + 512 * n, 512)]) for n in range(4)], dict(bias=False)),
        ("mix", [Panel([Block([("w_o_a", 0, 4, 256 * n, 256, 0, 0)]),
                        Block([("w_o_a", 4 * P, 2, 256 * n, 256, 0, 0), ("w_o_b", 0, 2, 256 * n, 256, 2, 0)])],
                       256, split_at=6) for n in range(4)], {}),
        ("add", [panel([("w_out", 512 * n, 512)], src="h", col=512 * n) for n in range(2)], {}),
        ("norm", [], dict(gain="norm2")),
        ("ffn", [], dict(gated=False, groups=[8] * 4)),
    ]
    w = "w_in_2"
    layer = [
        ("norm", [], dict(gain="norm_attn")),
        ("proj", [
            panel([(w, 0, 512)], rope=-1, dest="dq", tile0=0, query=True),
            panel([(w, 512, 512)], rope=-1, dest="dk", tile0=0),
            panel([(w, 1024, 512)], dest="dv", col=0)], dict(who="diff")),
        ("attend", [], dict(who="diff")),
        ("subln", [], {}),
        ("turn", [], dict(src="y_diff", tiles=4, tile0=0, gain="subln")),
        ("proj", [
            panel([(w, 1536, 512)], turn=True, dest="dq", tile0=0, query=True),
            panel([(w, 2048, 512)], turn=True, dest="dk", tile0=0),
            panel([(w, 2560, 512)], dest="dv", col=0)], dict(who="stick")),
        ("attend", [], dict(who="stick")),
        ("turn", [], dict(src="y_diff", tiles=4, tile0=4)),
        ("gates", [panel([(w, 3072 + 512 * n, 512)]) for n in range(4)], dict(bias=True)),
        ("mix", [Panel([Block([("w_o_diff_2", 0, 4, 256 * n, 256, 0, 0)]),
                        Block([("w_o_sb_2", 0, 4, 256 * n, 256, 0, 0)])], 256, split_at=4) for n in range(4)], {}),
        ("add", [panel([("w_out_2", 512 * n, 512)], src="h", col=512 * n) for n in range(2)], {}),
        ("norm", [], dict(gain="norm_ffn")),
        ("ffn", [], dict(gated=True, groups=[8, 8, 6])),
    ]
    for kind, panels, how in first + layer:
        if kind != "ffn":
            continue
        row = 0
        for g, kts in enumerate(how["groups"]):
            per = 2 if how["gated"] else 4
            for t in range(0, kts, per):
                c = (row + t) * P
                ps = [("w_ffn_in_2", c, 256), ("w_ffn_in_2", FF2 + c, 256)] if how["gated"] else [("w_up", c, 512)]
                panels.append(panel(ps, up=True, tile0=t, group=g, tiles=per))
            for n in range(2):
                m = "w_ffn_out_2" if how["gated"] else "w_down"
                panels.append(panel([(m, 512 * n, 512)], kts=kts, row=row * P, src="mid", col=512 * n, group=g))
            row += kts
    return first, layer


def attention_units(who):
    units, sets = [], 0
    for i in range(QT):
        w = (i + 1) * P
        diag = [(i * P, CAUSAL)]
        if who == "nsa":
            for h0 in range(0, NSA_HEADS, 2):
                for br in range(3):
                    for hh in range(2):
                        h = h0 + hh
                        units.append(dict(i=i, h=h, br=br, set=sets, slot=br * 2 + hh, size=6, vd=HD, head0=h0,
                                          width=CMP_PAD if br == 0 else w, j0=0, nj=1 if br == 0 else i + 1,
                                          masks=[(0, N_MASK + i)] if br == 0 else diag))
                sets += 1
        if who == "dil":
            for h0 in range(0, DIL_HPG, 2):
                for g in range(DIL_GROUPS):
                    for hh in range(2):
                        j0 = max(0, i - 1) if g == 0 else 0
                        off, own = ((BAND, CAUSAL), (MOD4, MOD4C), (MOD16, MOD16C))[g]
                        units.append(dict(i=i, h=g * DIL_HPG + h0 + hh, br=g, set=sets, slot=g * 2 + hh, size=6, vd=HD,
                                          head0=h0, width=(i + 1 - j0) * P, j0=j0, nj=i + 1 - j0,
                                          masks=[((j - j0) * P, own if j == i else off) for j in range(j0, i + 1)]))
                sets += 1
        if who == "diff":
            for h0 in range(0, 4, 2):
                for hh in range(2):
                    for c in range(2):
                        units.append(dict(i=i, h=(h0 + hh) * 2 + c, br=c, set=sets, slot=hh * 2 + c, size=4, vd=P,
                                          head0=h0, width=w, j0=0, nj=i + 1, masks=diag))
                sets += 1
        if who == "stick":
            for h in range(8):
                units.append(dict(i=i, h=h, br=0, set=sets, slot=h, size=8, vd=HD, head0=0,
                                  width=w, j0=0, nj=i + 1, masks=[(i * P, STRICT)]))
            sets += 1
    return units, sets


def build(nc, A, out):
    first, layer = make_plan()
    stages = first + layer

    blocks, n_split, n_direct = [], 0, 0
    layer_block0 = None
    for n, (kind, panels, how) in enumerate(stages):
        if n == len(first):
            layer_block0 = len(blocks)
        for p in panels:
            for b in p.blocks:
                b.raw = len(blocks)
                b.spl, b.direct = n_split, n_direct
                if b.split:
                    n_split += 1
                else:
                    n_direct += 1
                blocks.append(b)
        last = n == len(first) - 1 or n == len(stages) - 1 or stages[n + 1][0] == "compress"
        how["spl_ahead"] = n_split + (0 if last else SPLIT_RING)
    per_layer_blocks = len(blocks) - layer_block0
    assert per_layer_blocks % (RAW_RING * SPLIT_RING) == 0 and len(first) > 0

    def adds(stage):
        kind, panels, how = stage
        a = dict(stage_end=4)
        if kind == "norm":
            a.update(squares=QT, mean=1, root=1, scaled=QT, turned_ps=KT, split_hi=KT, split_lo=KT)
        if kind == "turn":
            a.update(turned_ps=how["tiles"], split_hi=how["tiles"], split_lo=how["tiles"])
        if kind == "proj":
            ropes = [p for p in panels if p.rope is not None]
            turns = [p for p in panels if p.rope is not None or p.turn]
            tiles = sum(turn_tiles(p) for p in turns)
            normed = [p for p in ropes if p.rope >= 0]
            a.update(staged=QT * len(panels), squares=len(normed), mean=len(normed), root=len(normed),
                     scaled=len(ropes), crossed=len(ropes), roped=len(ropes), turned_ps=tiles, turned=tiles)
        if kind == "compress":
            a.update(direct_used=4, hidden_ps=2, hidden=2, gate_arg=2, gate_sig=2, cmp_ps=2, cmp_v=1, mean=1, root=1,
                     roped=1, turned_ps=1, turned=1, cmp_bias=2)
        if kind == "attend":
            units, sets = attention_units(how["who"])
            n = len(units)
            a.update(scores=n, probs=n, probs_turned=n, pT_act=n // 2, pT_dve=n // 2, outs=n, combined=sets)
            if how["who"] == "stick":
                a.update(stick_scan=n, stick_weights=n)
            else:
                a.update(negmax=n)
            if how["who"] == "dil":
                a.update(lse_gap=sets, lse_exp=sets)
            if how["who"] == "diff":
                a.update(lam_dots=1, lam_exps=1)
        if kind == "subln":
            a.update(squares=1, mean=1, root=1, roped=1)
        if kind == "gates":
            a.update(gated=16)
        if kind == "mix":
            a.update(parts=8, mixed=8, split_hi=8, split_lo=8)
        if kind == "add":
            a.update(added=QT * len(panels))
        if kind == "ffn":
            ups = sum(p.tiles for p in panels if p.up)
            downs = len([p for p in panels if not p.up])
            a.update(acted=ups, mixed=ups, split_hi=ups, split_lo=ups, added=QT * downs)
        spl = sum(b.split for p in panels for b in p.blocks)
        a.update(split_blocks=spl)
        return a

    def turn_tiles(p):
        return p.width // HD if p.twice else p.width // P

    total, per_layer = {}, {}
    for n, st in enumerate(stages):
        st[2]["base"] = dict(total)
        for k, v in adds(st).items():
            total[k] = total.get(k, 0) + v
            if n >= len(first):
                per_layer[k] = per_layer.get(k, 0) + v

    def value(st, name, n, loop):
        v = st[2]["base"].get(name, 0) + n
        return v if loop is None else v + loop * per_layer[name]

    with ExitStack() as ctx:
        def sb(name, shape, dt=F32, scope=ctx):
            return scope.enter_context(nc.sbuf_tensor(name, shape, dt))

        def sem(name):
            return ctx.enter_context(nc.semaphore(name))

        x_sb = sb("x_sb", [P, QT, D])
        h_hi, h_lo = sb("h_hi", [P, KT, S], F32R), sb("h_lo", [P, KT, S], F32R)
        raw = sb("raw", [P, RAW_RING, BLK_COLS])
        w_hi = sb("w_hi", [P, SPLIT_RING, BLK_COLS], F32R)
        w_lo = sb("w_lo", [P, SPLIT_RING, BLK_COLS], F32R)
        tables = sb("tables", [P, C_ALL])
        masks = sb("masks", [P, M_ALL], BF16)
        ident_b = sb("ident_b", [P, P], BF16)
        gains = sb("gains", [P, 6, HD])
        gcos, gsin = sb("gcos", [P, QT, HD]), sb("gsin", [P, QT, HD])
        small = sb("small", [P, 192])
        gcol = sb("gcol", [P, 4, KT])
        bgate = sb("bgate", [P, 2 * KT])
        sub_col = sb("sub_col", [P, 4])
        pos_col = sb("pos_col", [P, 2, 16])
        w2_sb = sb("w2_sb", [P, 2, 2, HD])
        lam_in = sb("lam_in", [P, 4 * HD])
        lam_init = sb("lam_init", [P, 2])
        negmax_t = sb("negmax_t", [P, 2, 8])
        den_t = sb("den_t", [P, 2, 8])
        ident = tables[:, C_ID:C_ID + P]

        with ExitStack() as r:
            m_hi, m_lo = sb("m_hi", [P, KT, S], F32R, r), sb("m_lo", [P, KT, S], F32R, r)
        with ExitStack() as r:
            stage_s, stage_t = sb("stage_s", [P, QT, BANK], F32, r), sb("stage_t", [P, QT, BANK], F32, r)
            stage_u = sb("stage_u", [P, QT, BANK], F32, r)
        with ExitStack() as r:
            h_nat = sb("h_nat", [P, QT, D], F32, r)
            square_junk = sb("square_junk", [P, D], F32, r)
        with ExitStack() as r:
            nsa_bufs = (sb("nsa_probs", [P, 4, BANK], F32, r), sb("nsa_pT", [P, 2, BANK], F32, r),
                        sb("nsa_parts", [P, 512], F32, r))
        with ExitStack() as r:
            sb("m_hi_six", [P, 6, S], F32, r)
            dil_pT = sb("dil_pT", [P, 2, BANK], F32, r)
        with ExitStack() as r:
            sb("m_hi_first", [P, 4, S], F32, r)
            stick_rem = sb("stick_rem", [P, 2, BANK], F32, r)
            stick_after = sb("stick_after", [P, 2, BANK], F32, r)
        sb("mid_space", [P, 2 * KT * S])

        dest = {}
        with ExitStack() as r:
            dest["qa"], dest["ks"], dest["kw"] = (sb("q_nsa", [P, 6, S], F32, r), sb("k_slc", [P, 3, S], F32, r),
                                                  sb("k_win", [P, 3, S], F32, r))
            v_nsa, g_nsa = sb("v_nsa", [P, QT, 384], F32, r), sb("g_nsa", [P, QT, 36], F32, r)
            kc_T, vc = sb("kc_T", [P, 96], F32, r), sb("vc", [CMP_PAD, 3, HD], F32, r)
            with ExitStack() as r2:
                cmp_in = sb("cmp_in", [P, 6, S + 16], F32, r2)
                hid_z, hid_s, hid_h = (sb("hid_z", [P, 192], F32, r2), sb("hid_s", [P, 192], F32, r2),
                                       sb("hid_h", [P, 2, 192], F32, r2))
                cmp_b = sb("cmp_b", [P, 2, 2], F32, r2)
                kc_n, kc_t = sb("kc_n", [P, HD], F32, r2), sb("kc_t", [P, HD], F32, r2)
                kc_u = sb("kc_u", [P, 2 * HD], F32, r2)
            with ExitStack() as r2:
                y_nsa = sb("y_nsa", [P, QT, 768], F32, r2)
        with ExitStack() as r:
            dest["qb"], dest["kb"] = sb("q_dil", [P, 6, S], F32, r), sb("k_dil", [P, 6, S], F32, r)
            v_dil = sb("v_dil", [P, QT, 768], F32, r)
            with ExitStack() as r2:
                stage_dil = tuple(sb(f"stage_dil_{n}", [P, QT, 256], F32, r2) for n in "stu")
            with ExitStack() as r2:
                dil_bufs = (sb("dil_probs", [P, 4, BANK], F32, r2), dil_pT,
                            sb("dil_parts", [P, 512], F32, r2))
                y_dil = sb("y_dil", [P, QT, 256], F32, r2)
        with ExitStack() as r:
            dest["dq"], dest["dk"] = sb("q_two", [P, 4, S], F32, r), sb("k_two", [P, 4, S], F32, r)
            v_two = sb("v_two", [P, QT, 512], F32, r)
            two_bufs = (sb("two_probs", [P, 4, BANK], F32, r), sb("two_pT", [P, 2, BANK], F32, r),
                        sb("two_parts", [P, 512], F32, r))
            y_two = sb("y_two", [P, QT, 512], F32, r)
            stage_two = two_bufs[0]
        with ExitStack() as r:
            gate_T = sb("gate_T", [P, 16, S], F32, r)
            part_a, part_b = sb("part_a", [P, 2, S], F32, r), sb("part_b", [P, 2, S], F32, r)
        with ExitStack() as r:
            act_out, hid_m = sb("act_out", [P, 2, S], F32, r), sb("hid_m", [P, 2, S], F32, r)
            g_final, out_sb = sb("g_final", [P, D], F32, r), sb("out_sb", [P, QT, D], F32, r)
        with ExitStack() as r:
            mask_f = sb("mask_f", [P, M_ALL], F32, r)

        ps = [ctx.enter_context(nc.psum_tensor(f"bank{b}", [P, BANK], F32)) for b in range(8)]

        x_in, consts_in, col_in = sem("x_in"), sem("consts_in"), sem("col_in")
        landed = [sem(f"landed{i}") for i in range(RAW_RING)]
        w_hi_ready, w_lo_ready, products, direct_used = (sem("w_hi_ready"), sem("w_lo_ready"), sem("products"),
                                                         sem("direct_used"))
        stage_end = sem("stage_end")
        setup = sem("setup")
        names = ("squares mean root scaled turned_ps turned split_hi split_lo staged crossed roped hidden_ps hidden "
                 "gate_arg gate_sig cmp_ps cmp_v cmp_bias scores probs probs_turned pT_act pT_dve outs combined "
                 "stick_scan stick_weights negmax lse_gap lse_exp lam_dots lam_exps gated parts mixed added "
                 "acted out_ready").split()
        sm = {n: sem(n) for n in names}
        sm["stage_end"] = stage_end
        sm["direct_used"] = direct_used
        stored = sem("stored")
        block = ctx.enter_context(nc.Block())

        def staging(st):
            return dict(nsa=(stage_s, stage_t, stage_u), dil=stage_dil, diff=(stage_s, stage_t, stage_u),
                        stick=(None, None, stage_two))[st[2]["who"]]

        def of_blocks(n, scale, loop):
            return n * scale if loop is None else n * scale + loop * (per_layer_blocks * scale)

        def view(ring, slot, b):
            return ring[:, slot, 0:b.kts * b.width].rearrange("p (k n) -> p k n", k=b.kts)

        def raw_direct(b):
            return raw[:, b.raw % RAW_RING, :].rearrange("p (k n) -> p k n", k=8)

        landed_at = {}
        counts = [0] * RAW_RING
        for b in blocks:
            counts[b.raw % RAW_RING] += 16 * len(b.pieces)
            landed_at[b.raw] = counts[b.raw % RAW_RING]
        layer_landed = [sum(16 * len(b.pieces) for b in blocks[layer_block0:] if b.raw % RAW_RING == i)
                        for i in range(RAW_RING)]

        def landing(b, loop):
            return landed_at[b.raw] if loop is None else landed_at[b.raw] + loop * layer_landed[b.raw % RAW_RING]

        split_list = [b for b in blocks if b.split]

        class Splitter:

            def __init__(self, eng, which):
                self.eng, self.which, self.next = eng, which, 0

            def upto(self, st, n, loop):
                while self.next < min(n, st[2]["spl_ahead"]):
                    b = split_list[self.next]
                    slot = b.spl % SPLIT_RING
                    n_el = b.kts * b.width
                    if self.which == "hi":
                        self.eng.wait_ge(landed[b.raw % RAW_RING], landing(b, loop))
                        if b.spl >= SPLIT_RING:
                            self.eng.wait_ge(products, of_blocks(b.spl - SPLIT_RING + 1, 4, loop))
                        nc.scalar.activation(w_hi[:, slot, 0:n_el], raw[:, b.raw % RAW_RING, 0:n_el],
                                             ACT.Copy).then_inc(w_hi_ready, 1)
                    else:
                        self.eng.wait_ge(w_hi_ready, of_blocks(b.spl + 1, 1, loop))
                        nc.vector.tensor_tensor(w_lo[:, slot, 0:n_el], raw[:, b.raw % RAW_RING, 0:n_el],
                                                w_hi[:, slot, 0:n_el].bitcast(F32),
                                                ALU.subtract).then_inc(w_lo_ready, 1)
                    self.next += 1

        def last_block(p):
            return p.blocks[-1].spl

        def bank_count(p, q, loop):
            n = 4 * last_block(p) + q + 1
            return n if loop is None else n + loop * (4 * per_layer_blocks)

        def bank_set(k):
            return 4 * (k % 2)

        CONST_LOADS = 14
        LAYER_LOADS = 6

        def gain_col(st):
            return gcol[:, dict(norm1=0, norm2=1, norm_attn=2, norm_ffn=3)[st[2]["gain"]], :]

        def turn_gain(st):
            return (lambda t: sub_col[:, 1:2]) if st[2].get("gain") == "subln" else None

        def bufs(who):
            return dict(nsa=nsa_bufs, dil=dil_bufs, diff=two_bufs, stick=two_bufs)[who]

        def evac(eng, st, loop, units, t, pT, copy, args, name):
            u = units[t]
            eng.wait_ge(sm["probs_turned"], value(st, "probs_turned", t + 1, loop))
            if t >= 2:
                eng.wait_ge(sm["outs"], value(st, "outs", t - 1, loop))
            if u["width"] == CMP_PAD:
                o, i = pT[0:CMP_PAD, t % 2, 0:P], ps[4 + t % 2][0:CMP_PAD, 0:P]
            else:
                o, i = pT[:, t % 2, 0:u["nj"] * P], ps[4 + t % 2][:, 0:u["nj"] * P]
            copy(o, i, *args).then_inc(sm[name], 1)

        @block.sync
        def _(sp):
            sp.dma_start(x_sb[:, :, :], A["x"][0].rearrange("(i p) n -> p i n", p=P)).then_inc(x_in, 16)

            def loads(bs, loop):
                for b in bs:
                    prev = blocks[b.raw - RAW_RING] if b.raw >= RAW_RING else None
                    if prev is not None and prev.split:
                        sp.wait_ge(w_lo_ready, of_blocks(prev.spl + 1, 1, loop))
                    elif prev is not None:
                        sp.wait_ge(direct_used, prev.direct + 1)
                    dst = raw[:, b.raw % RAW_RING, 0:b.kts * b.width].rearrange("p (k n) -> p k n", k=b.kts)
                    for m, r0, kts, c0, n, k_at, c_at in b.pieces:
                        w = A[m][0] if loop is None else A[m][bass.ds(loop, 1)].rearrange("a r c -> (a r) c")
                        sp.dma_start(dst[:, k_at:k_at + kts, c_at:c_at + n],
                                     w[r0:r0 + kts * P, c0:c0 + n].rearrange("(k p) n -> p k n", p=P)
                                     ).then_inc(landed[b.raw % RAW_RING], 16)

            loads(blocks[:layer_block0], None)
            with sp.Fori(0, LAYERS) as loop:
                loads(blocks[layer_block0:], loop)
            sp.wait_ge(stored, 16 * QT)

        @block.scalar
        def _(act):
            spl = Splitter(act, "hi")

            def norm(st, loop):
                for i in range(QT):
                    if i:
                        act.wait_ge(sm["squares"], value(st, "squares", i, loop))
                    nc.scalar.activation(square_junk[:, :], x_sb[:, i, :], ACT.Square,
                                         accum_out=small[:, i:i + 1]).then_inc(sm["squares"], 1)
                act.wait_ge(sm["mean"], value(st, "mean", 1, loop))
                nc.scalar.activation(small[:, 4:8], small[:, 4:8], ACT.Sqrt).then_inc(sm["root"], 1)

            def turn(st, loop, hi, tiles, tile0, gain):
                for t in range(tiles):
                    act.wait_ge(sm["turned_ps"], value(st, "turned_ps", t + 1, loop))
                    nc.scalar.activation(hi[:, tile0 + t, :], ps[t % 8][:, :], ACT.Copy,
                                         scale=1.0 if gain is None else gain(t)).then_inc(sm["split_hi"], 1)

            def proj(st, loop):
                stage_s, stage_t, stage_u = staging(st)
                panels = st[1]
                staged, tp, n_root, n_roped = 0, 0, 0, 0
                pending = None

                def finish(p, tp):
                    for c in range(turn_tiles(p)):
                        act.wait_ge(sm["turned_ps"], value(st, "turned_ps", tp + c + 1, loop))
                        b = ps[p.set + c % 4]
                        if p.dest == "cmp_in":
                            c += p.tile0
                            nc.scalar.activation(cmp_in[0:HD, c, 0:S], b[0:HD, :], ACT.Copy)
                            nc.scalar.activation(cmp_in[HD:P, c, 0:S - 1], b[HD:P, 1:S],
                                                 ACT.Copy).then_inc(sm["turned"], 1)
                        else:
                            nc.scalar.activation(dest[p.dest][:, p.tile0 + c, :], b[:, :],
                                                 ACT.Copy).then_inc(sm["turned"], 1)
                    return tp + turn_tiles(p)

                for k, p in enumerate(panels):
                    p.set = bank_set(k)
                    spl.upto(st, last_block(p) + SPLIT_RING, loop)
                    roped = p.rope is not None
                    if roped and n_roped:
                        act.wait_ge(sm["roped"], value(st, "roped", n_roped, loop))
                    if p.turn and pending is not None:
                        act.wait_ge(sm["turned_ps"], value(st, "turned_ps", tp + turn_tiles(pending), loop))
                    for i in range(QT):
                        act.wait_ge(products, bank_count(p, i, loop))
                        b = ps[p.set + i]
                        if p.dest == "nsa_v":
                            nc.scalar.activation(v_nsa[:, i, :], b[:, 0:384], ACT.Copy)
                            ins = nc.scalar.activation(g_nsa[:, i, :], b[:, 384:420], ACT.Sigmoid)
                        elif p.dest in ("vb", "dv"):
                            to = v_dil if p.dest == "vb" else v_two
                            ins = nc.scalar.activation(to[:, i, p.col:p.col + p.width], b[:, 0:p.width], ACT.Copy)
                        elif p.twice and not roped:
                            heads = b[:, 0:p.width].rearrange("p (h d) -> p h d", d=HD)
                            pair = stage_u[:, i, 0:2 * p.width].rearrange("p (h c d) -> p h c d", c=2, d=HD)
                            nc.scalar.activation(pair[:, :, 0, :], heads, ACT.Copy)
                            ins = nc.scalar.activation(pair[:, :, 1, :], heads, ACT.Copy)
                        else:
                            to = stage_s if roped else stage_u
                            scale = HD ** -0.5 if p.query and not (roped and p.rope >= 0) else 1.0
                            ins = nc.scalar.activation(to[:, i, 0:p.width], b[:, 0:p.width], ACT.Copy, scale=scale)
                        ins.then_inc(sm["staged"], 1)
                    if pending is not None:
                        tp = finish(pending, tp)
                        pending = None
                    if roped:
                        n_roped += 1
                        if p.rope >= 0:
                            n_root += 1
                            act.wait_ge(sm["mean"], value(st, "mean", n_root, loop))
                            n = QT * p.width // HD
                            nc.scalar.activation(small[:, 32:32 + n], small[:, 0:n], ACT.Sqrt).then_inc(sm["root"], 1)
                    if roped or p.turn:
                        pending = p
                if pending is not None:
                    finish(pending, tp)

            def compress(st, loop):
                for kv in range(2):
                    act.wait_ge(sm["gate_arg"], value(st, "gate_arg", kv + 1, loop))
                    nc.scalar.activation(hid_s[:, :], hid_s[:, :], ACT.Sigmoid).then_inc(sm["gate_sig"], 1)
                act.wait_ge(sm["cmp_ps"], value(st, "cmp_ps", 2, loop))
                nc.scalar.activation(vc[:, :, :], ps[5][0:CMP_PAD, 0:192].rearrange("p (g d) -> p g d", g=3),
                                     ACT.Copy).then_inc(sm["cmp_v"], 1)
                act.wait_ge(sm["mean"], value(st, "mean", 1, loop))
                nc.scalar.activation(small[0:96, 1:2], small[0:96, 1:2], ACT.Sqrt).then_inc(sm["root"], 1)
                act.wait_ge(sm["turned_ps"], value(st, "turned_ps", 1, loop))
                nc.scalar.activation(kc_T[:, :], ps[6][:, 0:96], ACT.Copy).then_inc(sm["turned"], 1)

            def attend(st, loop):
                who = st[2]["who"]
                units, sets = attention_units(who)
                probs, pT, parts = bufs(who)
                if who == "diff":
                    act.wait_ge(sm["lam_dots"], value(st, "lam_dots", 1, loop))
                    nc.scalar.activation(small[:, 2:4], small[:, 0:2], ACT.Exp).then_inc(sm["lam_exps"], 1)
                for s in range(len(units) + 4):
                    if s < len(units):
                        u = units[s]
                        W, o = u["width"], u["set"]
                        src = ps[s % 4][:, 0:W]
                        if s >= 4:
                            act.wait_ge(sm["probs_turned"], value(st, "probs_turned", s - 3, loop))
                        if who == "stick":
                            if s >= 2:
                                act.wait_ge(sm["stick_scan"], value(st, "stick_scan", s - 1, loop))
                            act.wait_ge(sm["scores"], value(st, "scores", s + 1, loop))
                            nc.scalar.activation(probs[:, s % 4, 0:W], src, ACT.Sigmoid)
                            nc.scalar.activation(stick_rem[:, s % 2, 0:W], src, ACT.Sigmoid,
                                                 scale=-1.0).then_inc(sm["probs"], 1)
                        else:
                            if u["slot"] == 0 and o >= 2:
                                act.wait_ge(sm["combined"], value(st, "combined", o - 1, loop))
                            act.wait_ge(sm["negmax"], value(st, "negmax", s + 1, loop))
                            nc.scalar.activation(probs[:, s % 4, 0:W], src, ACT.Exp,
                                                 bias=negmax_t[:, o % 2, u["slot"]:u["slot"] + 1],
                                                 accum_out=den_t[:, o % 2, u["slot"]:u["slot"] + 1]
                                                 ).then_inc(sm["probs"], 1)
                    t = s - 2
                    if 0 <= t < len(units) and t % 2 == 0:
                        evac(act, st, loop, units, t, pT, nc.scalar.activation, (ACT.Copy,), "pT_act")
                    if who == "dil" and s >= 3 and s - 3 < len(units) and units[s - 3]["slot"] == 5:
                        o = units[s - 3]["set"]
                        act.wait_ge(sm["lse_gap"], value(st, "lse_gap", o + 1, loop))
                        nc.scalar.activation(small[:, 0:6], small[:, 0:6], ACT.Exp).then_inc(sm["lse_exp"], 1)

            def subln(st, loop):
                act.wait_ge(sm["mean"], value(st, "mean", 1, loop))
                nc.scalar.activation(small[:, 16:32], small[:, 16:32], ACT.Sqrt).then_inc(sm["root"], 1)

            def gates(st, loop):
                for k, p in enumerate(st[1]):
                    spl.upto(st, last_block(p) + SPLIT_RING, loop)
                    for q in range(4):
                        act.wait_ge(products, bank_count(p, q, loop))
                        t = 4 * k + q
                        nc.scalar.activation(gate_T[:, t, :], ps[bank_set(k) + q][:, :], ACT.Sigmoid,
                                             bias=bgate[:, t:t + 1] if st[2]["bias"] else 0.0
                                             ).then_inc(sm["gated"], 1)

            def mix(st, loop):
                for k, p in enumerate(st[1]):
                    spl.upto(st, last_block(p) + SPLIT_RING, loop)
                    for q in range(2):
                        t = 2 * k + q
                        act.wait_ge(sm["mixed"], value(st, "mixed", t + 1, loop))
                        nc.scalar.activation(h_hi[:, t, :], part_a[:, t % 2, :],
                                             ACT.Copy).then_inc(sm["split_hi"], 1)

            def add(st, loop):
                for p in st[1]:
                    spl.upto(st, last_block(p) + SPLIT_RING, loop)

            def ffn(st, loop):
                gated = st[2]["gated"]
                m = 0
                for k, p in enumerate(st[1]):
                    spl.upto(st, last_block(p) + SPLIT_RING, loop)
                    if not p.up:
                        continue
                    for q in range(p.tiles + 1):
                        if q < p.tiles:
                            t = m + q
                            if t >= 2:
                                act.wait_ge(sm["mixed"], value(st, "mixed", t - 1, loop))
                            act.wait_ge(products, bank_count(p, q, loop))
                            nc.scalar.activation(act_out[:, t % 2, :], ps[bank_set(k) + q][:, :],
                                                 ACT.Sigmoid if gated else ACT.Relu).then_inc(sm["acted"], 1)
                        if q >= 1:
                            t = m + q - 1
                            act.wait_ge(sm["mixed"], value(st, "mixed", t + 1, loop))
                            nc.scalar.activation(m_hi[:, p.tile0 + q - 1, :], hid_m[:, t % 2, :],
                                                 ACT.Copy).then_inc(sm["split_hi"], 1)
                    m += p.tiles

            def stage(st, loop):
                kind = st[0]
                if kind == "norm":
                    norm(st, loop)
                    turn(st, loop, h_hi, KT, 0, lambda t: gain_col(st)[:, t:t + 1])
                elif kind == "turn":
                    turn(st, loop, m_hi, st[2]["tiles"], st[2]["tile0"], turn_gain(st))
                else:
                    dict(proj=proj, compress=compress, attend=attend, subln=subln, gates=gates, mix=mix, add=add,
                         ffn=ffn)[kind](st, loop)
                spl.upto(st, st[2]["spl_ahead"], loop)
                act.drain().then_inc(stage_end, 1)
                act.wait_ge(sm["stage_end"], value(st, "stage_end", 4, loop))

            act.wait_ge(x_in, 16)
            act.wait_ge(consts_in, CONST_LOADS * 16)
            act.wait_ge(setup, 1)
            for st in first:
                stage(st, None)
            with act.Fori(0, LAYERS) as loop:
                act.wait_ge(col_in, loop * (16 * LAYER_LOADS) + 16 * LAYER_LOADS)
                for st in layer:
                    stage(st, loop)
            for i in range(QT):
                if i:
                    act.wait_ge(sm["squares"], total["squares"] + per_layer["squares"] + i)
                nc.scalar.activation(square_junk[:, :], x_sb[:, i, :], ACT.Square,
                                     accum_out=small[:, i:i + 1]).then_inc(sm["squares"], 1)
            act.wait_ge(sm["mean"], total["mean"] + per_layer["mean"] + 1)
            nc.scalar.activation(small[:, 4:8], small[:, 4:8], ACT.Sqrt).then_inc(sm["root"], 1)
            for i in range(QT):
                act.wait_ge(sm["out_ready"], i + 1)
                act.dma_start(out[0, i * P:(i + 1) * P, :], out_sb[:, i, :]).then_inc(stored, 16)

        @block.gpsimd
        def _(pool):
            def proj(st, loop):
                stage_s, stage_t, stage_u = staging(st)
                n_sq = n_rope = staged = 0
                for k, p in enumerate(st[1]):
                    staged += QT
                    if p.rope is None:
                        continue
                    s4 = stage_s[:, :, 0:p.width].rearrange("p i (h d) -> p i h d", d=HD)
                    t4 = stage_t[:, :, 0:p.width].rearrange("p i (h d) -> p i h d", d=HD)
                    if n_rope:
                        pool.wait_ge(sm["roped"], value(st, "roped", n_rope, loop))
                    pool.wait_ge(sm["staged"], value(st, "staged", staged, loop))
                    if p.rope >= 0:
                        n_sq += 1
                        nc.gpsimd.tensor_tensor(stage_t[:, :, 0:p.width], stage_s[:, :, 0:p.width],
                                                stage_s[:, :, 0:p.width], ALU.mult).then_inc(sm["squares"], 1)
                    n_rope += 1
                    pool.wait_ge(sm["scaled"], value(st, "scaled", n_rope, loop))
                    nh = p.width // HD
                    shape = [P, QT, nh, HALF]
                    nc.gpsimd.tensor_tensor(t4[:, :, :, 0:HALF], s4[:, :, :, HALF:HD],
                                            gsin[:, :, 0:HALF].unsqueeze(2).to_broadcast(shape), ALU.mult)
                    nc.gpsimd.tensor_tensor(t4[:, :, :, HALF:HD], s4[:, :, :, 0:HALF],
                                            gsin[:, :, HALF:HD].unsqueeze(2).to_broadcast(shape),
                                            ALU.mult).then_inc(sm["crossed"], 1)

            def attend(st, loop):
                units, _ = attention_units("stick")
                probs = bufs("stick")[0]
                for s, u in enumerate(units):
                    W = u["width"]
                    pool.wait_ge(sm["stick_scan"], value(st, "stick_scan", s + 1, loop))
                    nc.gpsimd.tensor_tensor(probs[:, s % 4, 0:W - 1], probs[:, s % 4, 0:W - 1],
                                            stick_after[:, s % 2, 1:W], ALU.mult).then_inc(sm["stick_weights"], 1)

            def mix(st, loop):
                for t in range(8):
                    pool.wait_ge(sm["parts"], value(st, "parts", t + 1, loop))
                    nc.gpsimd.tensor_tensor(part_a[:, t % 2, :], part_a[:, t % 2, :], part_b[:, t % 2, :],
                                            ALU.add).then_inc(sm["mixed"], 1)
                    pool.wait_ge(sm["split_hi"], value(st, "split_hi", t + 1, loop))
                    nc.gpsimd.tensor_tensor(h_lo[:, t, :], part_a[:, t % 2, :], h_hi[:, t, :].bitcast(F32),
                                            ALU.subtract).then_inc(sm["split_lo"], 1)

            def ffn(st, loop):
                t = 0
                for p in st[1]:
                    if not p.up:
                        continue
                    for q in range(p.tiles):
                        pool.wait_ge(sm["split_hi"], value(st, "split_hi", t + 1, loop))
                        nc.gpsimd.tensor_tensor(m_lo[:, p.tile0 + q, :], hid_m[:, t % 2, :],
                                                m_hi[:, p.tile0 + q, :].bitcast(F32),
                                                ALU.subtract).then_inc(sm["split_lo"], 1)
                        t += 1

            def stage(st, loop):
                f = dict(proj=proj, attend=attend, mix=mix, ffn=ffn).get(st[0])
                if f and not (st[0] == "attend" and st[2]["who"] != "stick") and not (st[0] == "proj" and st[2]["who"] == "stick"):
                    f(st, loop)
                    pool.drain().then_inc(stage_end, 1)
                else:
                    pool.sem_inc(stage_end, 1)
                pool.wait_ge(sm["stage_end"], value(st, "stage_end", 4, loop))

            pool.dma_start(tables[:, :], A["tables"]).then_inc(consts_in, 16)
            pool.dma_start(mask_f[:, :], A["masks"]).then_inc(consts_in, 16)
            for n, g in enumerate(("q_norm_a", "k_norm_cmp", "k_norm_slc", "k_norm_win", "q_norm_b", "k_norm_b")):
                pool.dma_start(gains[:, n, :], A[g].to_broadcast([P, HD])).then_inc(consts_in, 16)
            for n, g in enumerate(("norm1_g", "norm2_g")):
                pool.dma_start(gcol[:, n, :], A[g][0].rearrange("(k p) -> p k", p=P),
                               allow_slow_non_contiguous=True).then_inc(consts_in, 16)
            for n, g in enumerate(("cmp_k_pos", "cmp_v_pos")):
                pool.dma_start(pos_col[:, n, :],
                               A[g][0].rearrange("(k l) d -> (l d) k", l=2),
                               allow_slow_non_contiguous=True).then_inc(consts_in, 16)
            for n, g in enumerate(("cmp_k_w2", "cmp_v_w2")):
                pool.dma_start(w2_sb[:, n, :, :],
                               A[g][0].rearrange("(k p) n -> p k n", p=P)).then_inc(consts_in, 16)
            pool.wait_ge(consts_in, CONST_LOADS * 16)
            for st in first:
                stage(st, None)
            with pool.Fori(0, LAYERS) as loop:
                for dst, src in ((gcol[:, 2, :], "norm_attn_2"), (gcol[:, 3, :], "norm_ffn_2"),
                                 (bgate[:, :], "b_gate_2"), (sub_col[:, 0:1], "diff_subln_2")):
                    pool.dma_start(dst, A[src][bass.ds(loop, 1)].rearrange("a (k p) -> p (a k)", p=P),
                                   allow_slow_non_contiguous=True).then_inc(col_in, 16)
                pool.dma_start(lam_init[:, :],
                               A["lam_inits"][bass.ds(loop, 1)].to_broadcast([P, 2])).then_inc(col_in, 16)
                pool.dma_start(lam_in[:, :],
                               A["diff_lambda_2"][bass.ds(loop, 1)].rearrange("a r d -> a (r d)").to_broadcast(
                                   [P, 4 * HD])).then_inc(col_in, 16)
                for st in layer:
                    stage(st, loop)
            pool.dma_start(g_final[:, :], A["norm_final_2"].unsqueeze(0).to_broadcast([P, D])).then_inc(consts_in, 16)

        @block.vector
        def _(dve):
            spl = Splitter(dve, "lo")

            def turn(st, loop, hi, lo, tiles, tile0, gain):
                for t in range(tiles):
                    dve.wait_ge(sm["split_hi"], value(st, "split_hi", t + 1, loop))
                    nc.vector.scalar_tensor_tensor(lo[:, tile0 + t, :], ps[t % 8][:, :],
                                                   1.0 if gain is None else gain(t),
                                                   hi[:, tile0 + t, :].bitcast(F32), ALU.mult,
                                                   ALU.subtract).then_inc(sm["split_lo"], 1)

            def norm(st, loop):
                dve.wait_ge(sm["squares"], value(st, "squares", QT, loop))
                nc.vector.tensor_scalar(small[:, 4:8], small[:, 0:4], 1.0 / D, EPS, ALU.mult,
                                        ALU.add).then_inc(sm["mean"], 1)
                dve.wait_ge(sm["root"], value(st, "root", 1, loop))
                nc.vector.reciprocal(small[:, 0:4], small[:, 4:8])
                dve.drain()
                for i in range(QT):
                    nc.vector.tensor_scalar(h_nat[:, i, :], x_sb[:, i, :], small[:, i:i + 1], None,
                                            ALU.mult).then_inc(sm["scaled"], 1)

            def proj(st, loop):
                stage_s, stage_t, stage_u = staging(st)
                n_root, n_rope, staged, tiles, now, prev = 0, 0, 0, 0, None, None
                if st is first[1]:
                    nc.vector.memset(cmp_in[:, :, S - 1:S + 16], 0.0)
                for k, p in enumerate(st[1]):
                    spl.upto(st, last_block(p) + SPLIT_RING, loop)
                    staged += QT
                    if p.rope is None:
                        if p.turn:
                            tiles += turn_tiles(p)
                        continue
                    nh = p.width // HD
                    full = [P, QT, nh, HD]
                    s4 = stage_s[:, :, 0:p.width].rearrange("p i (h d) -> p i h d", d=HD)
                    t4 = stage_t[:, :, 0:p.width].rearrange("p i (h d) -> p i h d", d=HD)
                    r = small[:, 64:64 + QT * nh]
                    if p.rope != now:
                        cos = tables[:, C_COS:C_COS + QT * HD].rearrange("p (i d) -> p i d", i=QT)
                        sin = tables[:, C_SIN:C_SIN + QT * HD].rearrange("p (i d) -> p i d", i=QT)
                        if p.rope >= 0:
                            g = gains[:, p.rope, :]
                            nc.vector.tensor_tensor(gcos[:, :, :], cos,
                                                    g.unsqueeze(1).to_broadcast([P, QT, HD]), ALU.mult)
                            nc.vector.tensor_tensor(gsin[:, :, 0:HALF], sin[:, :, 0:HALF],
                                                    g[:, HALF:HD].unsqueeze(1).to_broadcast([P, QT, HALF]), ALU.mult)
                            nc.vector.tensor_tensor(gsin[:, :, HALF:HD], sin[:, :, HALF:HD],
                                                    g[:, 0:HALF].unsqueeze(1).to_broadcast([P, QT, HALF]), ALU.mult)
                        else:
                            nc.vector.tensor_copy(gcos[:, :, :], cos)
                            nc.vector.tensor_copy(gsin[:, :, :], sin)
                        now = p.rope
                        dve.drain()
                    if p.rope >= 0:
                        n_root += 1
                        dve.wait_ge(sm["squares"], value(st, "squares", n_root, loop))
                        nc.vector.tensor_reduce(small[:, 128:128 + QT * nh], t4, AX_X, ALU.add)
                        dve.drain()
                        a, b = (1.0, HD * EPS) if p.query else (1.0 / HD, EPS)
                        nc.vector.tensor_scalar(small[:, 0:QT * nh], small[:, 128:128 + QT * nh], a, b, ALU.mult,
                                                ALU.add).then_inc(sm["mean"], 1)
                        dve.wait_ge(sm["root"], value(st, "root", n_root, loop))
                        nc.vector.reciprocal(r, small[:, 32:32 + QT * nh])
                        dve.drain()
                        nc.vector.tensor_tensor(s4, s4, r.rearrange("p (i h) -> p i h", i=QT).unsqueeze(3)
                                                .to_broadcast(full), ALU.mult).then_inc(sm["scaled"], 1)
                        dve.drain()
                    else:
                        dve.wait_ge(sm["staged"], value(st, "staged", staged, loop))
                        dve.sem_inc(sm["scaled"], 1)
                    n_rope += 1
                    dve.wait_ge(sm["crossed"], value(st, "crossed", n_rope, loop))
                    nc.vector.tensor_tensor(s4, s4, gcos[:, :, :].unsqueeze(2).to_broadcast(full), ALU.mult)
                    dve.drain()
                    if prev is not None:
                        dve.wait_ge(sm["turned_ps"], value(st, "turned_ps", tiles, loop))
                    if p.twice:
                        for i in range(QT):
                            pair = stage_u[:, i, 0:2 * p.width].rearrange("p (h c d) -> p h c d", c=2, d=HD)
                            nc.vector.tensor_tensor(pair[:, :, 0, :], s4[:, i, :, :], t4[:, i, :, :], ALU.add)
                            ins = nc.vector.tensor_tensor(pair[:, :, 1, :], s4[:, i, :, :], t4[:, i, :, :], ALU.add)
                        ins.then_inc(sm["roped"], 1)
                    else:
                        nc.vector.tensor_tensor(stage_u[:, :, 0:p.width], stage_s[:, :, 0:p.width],
                                                stage_t[:, :, 0:p.width], ALU.add).then_inc(sm["roped"], 1)
                    prev = p
                    tiles += turn_tiles(p)

            def compress(st, loop):
                for kv in range(2):
                    dve.wait_ge(sm["hidden_ps"], value(st, "hidden_ps", kv + 1, loop))
                    for ht in range(2):
                        nc.vector.tensor_copy(cmp_b[:, kv, ht:ht + 1], ps[2 + ht][:, 0:1])
                    dve.drain()
                    for ht in range(2):
                        nc.vector.tensor_scalar(hid_z[:, ht * 96:ht * 96 + 96], ps[ht][:, 0:96],
                                                cmp_b[:, kv, ht:ht + 1], None, ALU.add)
                    dve.drain()
                    nc.vector.tensor_tensor(hid_s[:, :], hid_z[:, :], hid_z[:, :], ALU.mult)
                    dve.drain()
                    nc.vector.tensor_scalar(hid_s[:, :], hid_s[:, :], GELU_A * GELU_B, GELU_B, ALU.mult, ALU.add)
                    dve.drain()
                    nc.vector.tensor_tensor(hid_s[:, :], hid_s[:, :], hid_z[:, :],
                                            ALU.mult).then_inc(sm["gate_arg"], 1)
                    dve.wait_ge(sm["gate_sig"], value(st, "gate_sig", kv + 1, loop))
                    nc.vector.tensor_tensor(hid_h[:, kv, :], hid_s[:, :], hid_z[:, :],
                                            ALU.mult).then_inc(sm["hidden"], 1)
                dve.wait_ge(sm["cmp_ps"], value(st, "cmp_ps", 1, loop))
                n = slice(0, 96)
                nc.vector.tensor_copy(kc_n[n, :], ps[4][n, 0:HD])
                dve.drain()
                nc.vector.tensor_tensor(kc_t[n, :], kc_n[n, :], kc_n[n, :], ALU.mult)
                dve.drain()
                nc.vector.tensor_reduce(small[n, 0:1], kc_t[n, :], AX_X, ALU.add)
                dve.drain()
                nc.vector.tensor_scalar(small[n, 1:2], small[n, 0:1], 1.0 / HD, EPS, ALU.mult,
                                        ALU.add).then_inc(sm["mean"], 1)
                dve.wait_ge(sm["root"], value(st, "root", 1, loop))
                nc.vector.reciprocal(small[n, 2:3], small[n, 1:2])
                dve.drain()
                nc.vector.scalar_tensor_tensor(kc_n[n, :], kc_n[n, :], small[n, 2:3], gains[n, G_KC, :], ALU.mult,
                                               ALU.mult)
                dve.drain()
                nc.vector.tensor_tensor(kc_t[n, 0:HALF], kc_n[n, HALF:HD], tables[n, C_SINC:C_SINC + HALF], ALU.mult)
                nc.vector.tensor_tensor(kc_t[n, HALF:HD], kc_n[n, 0:HALF], tables[n, C_SINC + HALF:C_SINC + HD],
                                        ALU.mult)
                dve.drain()
                nc.vector.tensor_tensor(kc_n[n, :], kc_n[n, :], tables[n, C_COSC:C_COSC + HD], ALU.mult)
                dve.drain()
                nc.vector.tensor_tensor(kc_u[n, 0:HD], kc_n[n, :], kc_t[n, :], ALU.add)
                nc.vector.tensor_tensor(kc_u[n, HD:P], kc_n[n, :], kc_t[n, :], ALU.add).then_inc(sm["roped"], 1)
                shut = g_nsa[:, 0, :].rearrange("p (h b) -> p h b", b=3)[:, :, 0]
                nc.vector.tensor_scalar(shut, shut, tables[:, C_VALID:C_VALID + 1], None, ALU.mult)

            def combine(st, loop, who, u, half):
                o, i, h0, n = u["set"], u["i"], u["head0"], u["size"]
                probs, pT, parts = bufs(who)
                bank, den, nm = ps[6 + o % 2], den_t[:, o % 2, :], negmax_t[:, o % 2, :]
                w = small[:, 16:22]
                if who == "dil" and half == 0:
                    nc.vector.tensor_reduce(small[:, 8:10], nm[:, 0:6].rearrange("p (g h) -> p h g", g=3), AX_X,
                                            ALU.min)
                    dve.drain()
                    nc.vector.tensor_tensor(small[:, 0:6].rearrange("p (g h) -> p g h", g=3),
                                            small[:, 8:10].unsqueeze(1).to_broadcast([P, 3, 2]),
                                            nm[:, 0:6].rearrange("p (g h) -> p g h", g=3),
                                            ALU.subtract).then_inc(sm["lse_gap"], 1)
                    return
                dve.wait_ge(sm["outs"], value(st, "outs", u["last"] + 1, loop))
                if who == "stick":
                    nc.vector.tensor_copy(y_two[:, i, :], bank[:, :]).then_inc(sm["combined"], 1)
                    return
                if who == "nsa":
                    nc.vector.reciprocal(small[:, 10:16], den[:, 0:6])
                    dve.drain()
                    nc.vector.tensor_tensor(w.rearrange("p (b h) -> p b h", b=3),
                                            small[:, 10:16].rearrange("p (b h) -> p b h", b=3),
                                            g_nsa[:, i, 3 * h0:3 * h0 + 6].rearrange("p (h b) -> p b h", b=3),
                                            ALU.mult)
                if who == "dil":
                    dve.wait_ge(sm["lse_exp"], value(st, "lse_exp", o + 1, loop))
                    nc.vector.tensor_tensor(small[:, 24:30], small[:, 0:6], den[:, 0:6], ALU.mult)
                    dve.drain()
                    nc.vector.tensor_reduce(small[:, 30:32], small[:, 24:30].rearrange("p (g h) -> p h g", g=3), AX_X,
                                            ALU.add)
                    dve.drain()
                    nc.vector.reciprocal(small[:, 32:34], small[:, 30:32])
                    dve.drain()
                    nc.vector.tensor_tensor(w.rearrange("p (g h) -> p g h", g=3),
                                            small[:, 0:6].rearrange("p (g h) -> p g h", g=3),
                                            small[:, 32:34].unsqueeze(1).to_broadcast([P, 3, 2]), ALU.mult)
                if who == "diff":
                    nc.vector.reciprocal(w[:, 0:4], den[:, 0:4])
                    dve.drain()
                    odd = w[:, 1:4:2]
                    nc.vector.tensor_scalar(odd, odd, sub_col[:, 2:3], None, ALU.mult)
                dve.drain()
                cols = n * u["vd"]
                nc.vector.tensor_tensor(parts[:, 0:cols].rearrange("p (n d) -> p n d", n=n),
                                        bank[:, 0:cols].rearrange("p (n d) -> p n d", n=n),
                                        w[:, 0:n].unsqueeze(2).to_broadcast([P, n, u["vd"]]),
                                        ALU.mult).then_inc(sm["combined"], 1)
                dve.drain()
                if who == "diff":
                    pr = parts[:, 0:512].rearrange("p (h c d) -> p h c d", h=2, c=2)
                    nc.vector.tensor_tensor(y_two[:, i, h0 * P:(h0 + 2) * P].rearrange("p (h d) -> p h d", h=2),
                                            pr[:, :, 0, :], pr[:, :, 1, :], ALU.add)
                    return
                y = (y_nsa if who == "nsa" else y_dil)[:, i, h0 * HD:(h0 + 2) * HD]
                nc.vector.tensor_tensor(y, parts[:, 0:128], parts[:, 128:256], ALU.add)
                dve.drain()
                nc.vector.tensor_tensor(y, y, parts[:, 256:384], ALU.add)

            def attend(st, loop):
                who = st[2]["who"]
                units, sets = attention_units(who)
                pT = bufs(who)[1]
                last = {u["set"]: s for s, u in enumerate(units)}
                for u in units:
                    u["last"] = last[u["set"]]
                if who == "diff":
                    lam = lam_in[:, :].rearrange("p (a b d) -> p a b d", a=2, b=2)
                    prod = bufs(who)[2][:, 0:2 * HD].rearrange("p (a d) -> p a d", a=2)
                    nc.vector.tensor_tensor(prod, lam[:, :, 0, :], lam[:, :, 1, :], ALU.mult)
                    dve.drain()
                    nc.vector.tensor_reduce(small[:, 0:2], prod, AX_X, ALU.add).then_inc(sm["lam_dots"], 1)
                    dve.wait_ge(sm["lam_exps"], value(st, "lam_exps", 1, loop))
                    nc.vector.tensor_tensor(sub_col[:, 3:4], small[:, 3:4], small[:, 2:3], ALU.subtract)
                    dve.drain()
                    nc.vector.tensor_tensor(sub_col[:, 2:3], sub_col[:, 3:4], lam_init[:, 0:1], ALU.subtract)
                    nc.vector.tensor_tensor(sub_col[:, 1:2], sub_col[:, 0:1], lam_init[:, 1:2], ALU.mult)
                    dve.drain()
                for s in range(len(units) + 5):
                    if s < len(units):
                        u = units[s]
                        W, o = u["width"], u["set"]
                        if who == "stick":
                            dve.wait_ge(sm["probs"], value(st, "probs", s + 1, loop))
                            if s >= 2:
                                dve.wait_ge(sm["stick_weights"], value(st, "stick_weights", s - 1, loop))
                            rem = stick_rem[:, s % 2, 0:W][:, ::-1]
                            nc.vector.tensor_tensor_scan(stick_after[:, s % 2, 0:W][:, ::-1], rem, rem, 1.0,
                                                         ALU.mult, ALU.min).then_inc(sm["stick_scan"], 1)
                        else:
                            dve.wait_ge(sm["scores"], value(st, "scores", s + 1, loop))
                            nc.vector.tensor_reduce(negmax_t[:, o % 2, u["slot"]:u["slot"] + 1], ps[s % 4][:, 0:W],
                                                    AX_X, ALU.max, negate=True).then_inc(sm["negmax"], 1)
                    t = s - 2
                    if 0 <= t < len(units) and t % 2 == 1:
                        evac(dve, st, loop, units, t, pT, nc.vector.tensor_copy, (), "pT_dve")
                    if who == "dil" and 0 <= s - 2 < len(units) and units[s - 2]["slot"] == 5:
                        combine(st, loop, who, units[s - 2], 0)
                    c = s - 4
                    if 0 <= c < len(units) and c == units[c]["last"]:
                        combine(st, loop, who, units[c], 1)

            def subln(st, loop):
                sq = bufs("diff")[0][:, :, :].rearrange("p a b -> p (a b)")
                y = y_two[:, :, :].rearrange("p i n -> p (i n)")
                nc.vector.tensor_tensor(sq, y, y, ALU.mult)
                dve.drain()
                nc.vector.tensor_reduce(small[:, 0:16], sq.rearrange("p (n d) -> p n d", d=P), AX_X,
                                        ALU.add).then_inc(sm["squares"], 1)
                dve.drain()
                nc.vector.tensor_scalar(small[:, 16:32], small[:, 0:16], 1.0 / P, EPS, ALU.mult,
                                        ALU.add).then_inc(sm["mean"], 1)
                dve.wait_ge(sm["root"], value(st, "root", 1, loop))
                nc.vector.reciprocal(small[:, 32:48], small[:, 16:32])
                dve.drain()
                y3 = y.rearrange("p (n d) -> p n d", d=P)
                nc.vector.tensor_tensor(y3, y3, small[:, 32:48].unsqueeze(2).to_broadcast([P, 16, P]),
                                        ALU.mult).then_inc(sm["roped"], 1)

            def gates(st, loop):
                for p in st[1]:
                    spl.upto(st, last_block(p) + SPLIT_RING, loop)

            def mix(st, loop):
                for k, p in enumerate(st[1]):
                    spl.upto(st, last_block(p) + SPLIT_RING, loop)
                    dve.wait_ge(products, bank_count(p, 3, loop))
                    for q in range(2):
                        t = 2 * k + q
                        if t >= 2:
                            dve.wait_ge(sm["split_lo"], value(st, "split_lo", t - 1, loop))
                        nc.vector.tensor_tensor(part_a[:, t % 2, :], ps[bank_set(k) + q][:, :], gate_T[:, t, :],
                                                ALU.mult)
                        nc.vector.tensor_tensor(part_b[:, t % 2, :], ps[bank_set(k) + 2 + q][:, :],
                                                gate_T[:, 8 + t, :], ALU.mult).then_inc(sm["parts"], 1)

            def add_panel(st, k, p, loop):
                for i in range(QT):
                    dve.wait_ge(products, bank_count(p, i, loop))
                    xs = x_sb[:, i, p.col:p.col + BANK]
                    nc.vector.tensor_tensor(xs, xs, ps[bank_set(k) + i][:, :], ALU.add).then_inc(sm["added"], 1)

            def add(st, loop):
                for k, p in enumerate(st[1]):
                    spl.upto(st, last_block(p) + SPLIT_RING, loop)
                    add_panel(st, k, p, loop)

            def ffn(st, loop):
                gated = st[2]["gated"]
                m = 0
                for k, p in enumerate(st[1]):
                    spl.upto(st, last_block(p) + SPLIT_RING, loop)
                    if not p.up:
                        if k and not st[1][k - 1].up and st[1][k - 1].group != p.group:
                            pass
                        add_panel(st, k, p, loop)
                        continue
                    if gated:
                        dve.wait_ge(products, bank_count(p, 3, loop))
                    for q in range(p.tiles):
                        t = m + q
                        if t >= 2:
                            dve.wait_ge(sm["split_lo"], value(st, "split_lo", t - 1, loop))
                        dve.wait_ge(sm["acted"], value(st, "acted", t + 1, loop))
                        a, b = act_out[:, t % 2, :], ps[bank_set(k) + q][:, :]
                        if gated:
                            nc.vector.tensor_tensor(hid_m[:, t % 2, :], b, a, ALU.mult)
                            dve.drain()
                            nc.vector.tensor_tensor(hid_m[:, t % 2, :], ps[bank_set(k) + 2 + q][:, :],
                                                    hid_m[:, t % 2, :], ALU.mult).then_inc(sm["mixed"], 1)
                        else:
                            nc.vector.scalar_tensor_tensor(hid_m[:, t % 2, :], b, 0.0, a, ALU.max,
                                                           ALU.mult).then_inc(sm["mixed"], 1)
                    m += p.tiles

            def stage(st, loop):
                kind = st[0]
                if kind == "norm":
                    norm(st, loop)
                    turn(st, loop, h_hi, h_lo, KT, 0, lambda t: gain_col(st)[:, t:t + 1])
                elif kind == "turn":
                    turn(st, loop, m_hi, m_lo, st[2]["tiles"], st[2]["tile0"], turn_gain(st))
                else:
                    dict(proj=proj, compress=compress, attend=attend, subln=subln, gates=gates, mix=mix, add=add,
                         ffn=ffn)[kind](st, loop)
                spl.upto(st, st[2]["spl_ahead"], loop)
                dve.drain().then_inc(stage_end, 1)
                dve.wait_ge(sm["stage_end"], value(st, "stage_end", 4, loop))

            dve.wait_ge(x_in, 16)
            dve.wait_ge(consts_in, CONST_LOADS * 16)
            nc.vector.tensor_copy(ident_b[:, :], ident)
            nc.vector.tensor_copy(masks[:, :], mask_f[:, :])
            dve.drain().then_inc(setup, 1)
            for st in first:
                stage(st, None)
            with dve.Fori(0, LAYERS) as loop:
                dve.wait_ge(col_in, loop * (16 * LAYER_LOADS) + 16 * LAYER_LOADS)
                for st in layer:
                    stage(st, loop)
            dve.wait_ge(sm["squares"], total["squares"] + per_layer["squares"] + QT)
            nc.vector.tensor_scalar(small[:, 4:8], small[:, 0:4], 1.0 / D, EPS, ALU.mult,
                                    ALU.add).then_inc(sm["mean"], 1)
            dve.wait_ge(sm["root"], total["root"] + per_layer["root"] + 1)
            nc.vector.reciprocal(small[:, 0:4], small[:, 4:8])
            dve.drain()
            dve.wait_ge(consts_in, CONST_LOADS * 16 + 16)
            for i in range(QT):
                nc.vector.scalar_tensor_tensor(out_sb[:, i, :], x_sb[:, i, :], small[:, i:i + 1], g_final[:, :],
                                               ALU.mult, ALU.mult).then_inc(sm["out_ready"], 1)

        @block.tensor
        def _(pe):
            def turn(st, loop, src, tiles):
                for t in range(tiles):
                    if t >= 8:
                        pe.wait_ge(sm["split_lo"], value(st, "split_lo", t - 7, loop))
                    for i in range(QT):
                        if st[0] == "norm" and t == 0:
                            pe.wait_ge(sm["scaled"], value(st, "scaled", i + 1, loop))
                        ins = nc.tensor.transpose(ps[t % 8][:, i * P:(i + 1) * P], src[:, i, t * P:(t + 1) * P], ident)
                    ins.then_inc(sm["turned_ps"], 1)

            def multiply(p, b, k_at, base, x_hi, x_lo, natural, loop, outs=4, width=None, begin=None, end=None, inc=1):
                slot = b.spl % SPLIT_RING
                hi, lo = view(w_hi, slot, b), view(w_lo, slot, b)
                for q in range(outs):
                    for k in range(b.kts):
                        kt = k_at + k
                        n = slice(q * P, (q + 1) * P)
                        if natural:
                            o = ps[base + q][:, 0:b.width]
                            ops = ((x_hi[:, kt, n], hi[:, k, :]), (x_hi[:, kt, n], lo[:, k, :]),
                                   (x_lo[:, kt, n], hi[:, k, :]))
                        else:
                            o = ps[base + q][:, :]
                            ops = ((hi[:, k, n], x_hi[:, kt, :]), (hi[:, k, n], x_lo[:, kt, :]),
                                   (lo[:, k, n], x_hi[:, kt, :]))
                        for e, (l, r) in enumerate(ops):
                            ins = nc.tensor.matmul(o, l, r, start=(kt == 0 and e == 0),
                                                   stop=(kt == p.kts - 1 and e == 2))
                    ins.then_inc(products, 1)

            def gemm(st, p, base, x_hi, x_lo, natural, loop, before=None):
                k_at = 0
                for b in p.blocks:
                    pe.wait_ge(w_lo_ready, of_blocks(b.spl + 1, 1, loop))
                    multiply(p, b, k_at, base, x_hi, x_lo, natural, loop)
                    k_at += b.kts

            def proj(st, loop):
                stage_s, stage_t, stage_u = staging(st)
                tiles, staged, ropes, pending = 0, 0, 0, None
                released = {}

                def turn_panel(p):
                    nonlocal tiles
                    if p.rope is not None:
                        pe.wait_ge(sm["roped"], value(st, "roped", p.roped_at, loop))
                    else:
                        pe.wait_ge(sm["staged"], value(st, "staged", p.staged_at, loop))
                    for c in range(turn_tiles(p)):
                        if c >= 4:
                            pe.wait_ge(sm["turned"], value(st, "turned", tiles - 3, loop))
                        for i in range(QT):
                            src = stage_u[:, i, c * P:(c + 1) * P]
                            ins = nc.tensor.transpose(ps[p.set + c % 4][:, i * P:(i + 1) * P], src, ident)
                        ins.then_inc(sm["turned_ps"], 1)
                        tiles += 1
                    released[p.set] = tiles

                for k, p in enumerate(st[1]):
                    p.set = bank_set(k)
                    staged += QT
                    p.staged_at = staged
                    if p.rope is not None:
                        ropes += 1
                        p.roped_at = ropes
                    if k >= 2:
                        pe.wait_ge(sm["staged"], value(st, "staged", staged - 2 * QT, loop))
                    if released.get(p.set):
                        pe.wait_ge(sm["turned"], value(st, "turned", released[p.set], loop))
                    gemm(st, p, p.set, h_hi, h_lo, True, loop)
                    if pending is not None:
                        turn_panel(pending)
                        pending = None
                    if p.rope is not None or p.turn:
                        pending = p
                if pending is not None:
                    turn_panel(pending)

            def compress(st, loop):
                b0 = st[1][0].blocks
                for kv in range(2):
                    if kv:
                        pe.wait_ge(sm["hidden"], value(st, "hidden", 1, loop))
                    for half in range(2):
                        b = b0[2 * kv + half]
                        pe.wait_ge(landed[b.raw % RAW_RING], landing(b, loop))
                        w = raw_direct(b)
                        for ht in range(2):
                            for k in range(8):
                                kt = half * 8 + k
                                x = cmp_in[:, 3 * kv:3 * kv + 3, 2 * kt:2 * kt + 16 * 31 + 1:16]
                                nc.tensor.matmul(ps[ht][:, 0:96].rearrange("p (g c) -> p g c", g=3),
                                                 w[:, k, ht * P:(ht + 1) * P], x, start=kt == 0, stop=kt == 15)
                                ins = nc.tensor.matmul(ps[2 + ht][:, 0:1], w[:, k, ht * P:(ht + 1) * P],
                                                       pos_col[:, kv, kt:kt + 1], start=kt == 0, stop=kt == 15)
                        ins.then_inc(direct_used, 1)
                    ins = nc.tensor.matmul(ps[7][0:2, 0:2], ident[:, 0:2], ident[:, 0:2], start=True, stop=True)
                    ins.then_inc(sm["hidden_ps"], 1)
                pe.wait_ge(sm["hidden"], value(st, "hidden", 1, loop))
                for ht in range(2):
                    ins = nc.tensor.matmul(ps[4][0:96, 0:HD], hid_h[:, 0, ht * 96:ht * 96 + 96], w2_sb[:, 0, ht, :],
                                           start=ht == 0, stop=ht == 1)
                ins.then_inc(sm["cmp_ps"], 1)
                pe.wait_ge(sm["hidden"], value(st, "hidden", 2, loop))
                for g in range(3):
                    for ht in range(2):
                        ins = nc.tensor.matmul(ps[5][0:CMP_PAD, g * HD:(g + 1) * HD],
                                               hid_h[:, 1, ht * 96 + g * 32:ht * 96 + g * 32 + 32], w2_sb[:, 1, ht, :],
                                               start=ht == 0, stop=ht == 1)
                ins.then_inc(sm["cmp_ps"], 1)
                pe.wait_ge(sm["roped"], value(st, "roped", 1, loop))
                nc.tensor.transpose(ps[6][:, 0:96], kc_u[0:96, :],
                                    ident[0:96, 0:96]).then_inc(sm["turned_ps"], 1)

            def operands(who, u):
                i, h, br = u["i"], u["h"], u["br"]
                r = slice(HD * (h % 2), HD * (h % 2) + HD)
                n, kn = slice(i * P, (i + 1) * P), slice(u["j0"] * P, (i + 1) * P)
                if who == "nsa":
                    g = h // (NSA_HEADS // NSA_GROUPS)
                    q = dest["qa"][r, h // 2, n]
                    if br == 0:
                        return q, kc_T[r, g * CMP_PAD:(g + 1) * CMP_PAD], lambda j: vc[:, g, :]
                    k = dest["ks" if br == 1 else "kw"][r, g, kn]
                    c = 192 * (br - 1) + g * HD
                    return q, k, lambda j: v_nsa[:, j, c:c + HD]
                if who == "dil":
                    return (dest["qb"][r, h // 2, n], dest["kb"][r, h // 2, kn],
                            lambda j: v_dil[:, j, h * HD:(h + 1) * HD])
                c = (h // 2) * P if who == "diff" else h * HD
                return dest["dq"][r, h // 2, n], dest["dk"][r, h // 2, kn], lambda j: v_two[:, j, c:c + u["vd"]]

            def attend(st, loop):
                who = st[2]["who"]
                units, sets = attention_units(who)
                probs, pT, _ = bufs(who)
                for s in range(len(units) + 3):
                    if s < len(units):
                        u = units[s]
                        q, k, _v = operands(who, u)
                        if s >= 4:
                            pe.wait_ge(sm["probs"], value(st, "probs", s - 3, loop))
                        nc.tensor.matmul(ps[s % 4][:, 0:u["width"]], q, k, start=True, stop=False)
                        for n, (c, m) in enumerate(u["masks"]):
                            wdt = CMP_PAD if m >= N_MASK else P
                            m0 = m * P if m < N_MASK else N_MASK * P + (m - N_MASK) * CMP_PAD
                            ins = nc.tensor.matmul(ps[s % 4][:, c:c + wdt], ident_b[:, :], masks[:, m0:m0 + wdt],
                                                   start=False, stop=n == len(u["masks"]) - 1)
                        ins.then_inc(sm["scores"], 1)
                    t = s - 2
                    if 0 <= t < len(units):
                        u = units[t]
                        if who == "stick":
                            pe.wait_ge(sm["stick_weights"], value(st, "stick_weights", t + 1, loop))
                        else:
                            pe.wait_ge(sm["probs"], value(st, "probs", t + 1, loop))
                        if t >= 2:
                            if t % 2:
                                pe.wait_ge(sm["pT_dve"], value(st, "pT_dve", t // 2, loop))
                            else:
                                pe.wait_ge(sm["pT_act"], value(st, "pT_act", t // 2, loop))
                        for j in range(u["nj"]):
                            if u["width"] == CMP_PAD:
                                ins = nc.tensor.transpose(ps[4 + t % 2][0:CMP_PAD, 0:P], probs[:, t % 4, 0:CMP_PAD],
                                                          ident)
                            else:
                                ins = nc.tensor.transpose(ps[4 + t % 2][:, j * P:(j + 1) * P],
                                                          probs[:, t % 4, j * P:(j + 1) * P], ident)
                        ins.then_inc(sm["probs_turned"], 1)
                    v = s - 3
                    if 0 <= v < len(units):
                        u = units[v]
                        values = operands(who, u)[2]
                        if v % 2:
                            pe.wait_ge(sm["pT_dve"], value(st, "pT_dve", v // 2 + 1, loop))
                        else:
                            pe.wait_ge(sm["pT_act"], value(st, "pT_act", v // 2 + 1, loop))
                        if u["slot"] == 0 and u["set"] >= 2:
                            pe.wait_ge(sm["combined"], value(st, "combined", u["set"] - 1, loop))
                        o = ps[6 + u["set"] % 2][:, u["slot"] * u["vd"]:(u["slot"] + 1) * u["vd"]]
                        for j in range(u["nj"]):
                            l = pT[0:CMP_PAD, v % 2, 0:P] if u["width"] == CMP_PAD else pT[:, v % 2, j * P:(j + 1) * P]
                            ins = nc.tensor.matmul(o, l, values(u["j0"] + j), start=j == 0, stop=j == u["nj"] - 1)
                        ins.then_inc(sm["outs"], 1)

            def gates(st, loop):
                for k, p in enumerate(st[1]):
                    if k >= 2:
                        pe.wait_ge(sm["gated"], value(st, "gated", 4 * (k - 1), loop))
                    gemm(st, p, bank_set(k), h_hi, h_lo, False, loop)

            def mix(st, loop):
                for k, p in enumerate(st[1]):
                    cut, k_at, base = p.split_at, 0, bank_set(k)
                    if k >= 2:
                        pe.wait_ge(sm["parts"], value(st, "parts", 2 * (k - 1), loop))
                    for b in p.blocks:
                        pe.wait_ge(w_lo_ready, of_blocks(b.spl + 1, 1, loop))
                        slot = b.spl % SPLIT_RING
                        hi, lo = view(w_hi, slot, b), view(w_lo, slot, b)
                        parts = [(0, 0, cut), (2, cut, KT)]
                        parts = [(o, max(a, k_at), min(e, k_at + b.kts), a, e) for o, a, e in parts]
                        parts = [x for x in parts if x[1] < x[2]]
                        for o, ka, kb, a, e in parts:
                            for q in range(2):
                                n = slice(q * P, (q + 1) * P)
                                for kt in range(ka, kb):
                                    kk = kt - k_at
                                    ops = ((hi[:, kk, n], m_hi[:, kt, :]), (hi[:, kk, n], m_lo[:, kt, :]),
                                           (lo[:, kk, n], m_hi[:, kt, :]))
                                    for m, (l, r) in enumerate(ops):
                                        ins = nc.tensor.matmul(ps[base + o + q][:, :], l, r,
                                                               start=(kt == a and m == 0),
                                                               stop=(kt == e - 1 and m == 2))
                                ins.then_inc(products, 4 // (2 * len(parts)))
                        k_at += b.kts

            def add(st, loop):
                for k, p in enumerate(st[1]):
                    gemm(st, p, bank_set(k), h_hi, h_lo, True, loop)

            def ffn(st, loop):
                done = {"up": 0, "down": 0}
                readers = []
                for k, p in enumerate(st[1]):
                    if k >= 2:
                        pe.wait_ge(sm[readers[k - 2][0]], value(st, *readers[k - 2], loop))
                    if p.up:
                        done["up"] += p.tiles
                        readers.append(("mixed", done["up"]))
                        gemm(st, p, bank_set(k), h_hi, h_lo, False, loop)
                    else:
                        pe.wait_ge(sm["split_lo"], value(st, "split_lo", done["up"], loop))
                        done["down"] += QT
                        readers.append(("added", done["down"]))
                        gemm(st, p, bank_set(k), m_hi, m_lo, True, loop)

            def stage(st, loop):
                kind = st[0]
                if kind == "norm":
                    turn(st, loop, h_nat, KT)
                elif kind == "turn":
                    turn(st, loop, dict(y_nsa=y_nsa, y_dil=y_dil, y_diff=y_two)[st[2]["src"]], st[2]["tiles"])
                elif kind != "subln":
                    dict(proj=proj, compress=compress, attend=attend, gates=gates, mix=mix, add=add,
                         ffn=ffn)[kind](st, loop)
                if kind == "subln":
                    pe.sem_inc(stage_end, 1)
                else:
                    pe.drain().then_inc(stage_end, 1)
                pe.wait_ge(sm["stage_end"], value(st, "stage_end", 4, loop))

            pe.wait_ge(consts_in, CONST_LOADS * 16)
            pe.wait_ge(setup, 1)
            for st in first:
                stage(st, None)
            with pe.Fori(0, LAYERS) as loop:
                for st in layer:
                    stage(st, loop)


def shape_tables():
    import numpy as np

    half = np.arange(HALF, dtype=np.float32)
    inv = np.power(np.float32(10000.0), -half / np.float32(HALF)).astype(np.float32)

    def cos_sin(pos):
        ang = pos.astype(np.float32)[:, None] * inv[None, :]
        c, s = np.cos(ang), np.sin(ang)
        return np.concatenate([c, c], 1), np.concatenate([-s, s], 1)

    tables = np.zeros((P, C_ALL), np.float32)
    c, s = cos_sin(np.arange(S))
    tables[:, C_COS:C_COS + 256] = c.reshape(QT, P, HD).transpose(1, 0, 2).reshape(P, 256)
    tables[:, C_SIN:C_SIN + 256] = s.reshape(QT, P, HD).transpose(1, 0, 2).reshape(P, 256)
    c_end = np.arange(CMP_PAD) * CMP_STRIDE + CMP_LEN - 1
    c, s = cos_sin(c_end)
    tables[0:96, C_COSC:C_COSC + HD] = np.tile(c, (3, 1))
    tables[0:96, C_SINC:C_SINC + HD] = np.tile(s, (3, 1))
    tables[:, C_VALID] = np.arange(P) >= CMP_LEN - 1
    tables[:, C_ID:C_ID + P] = np.eye(P)
    q, k = np.arange(P)[:, None], np.arange(P)[None, :]
    m4, m16, causal = (q - k) % 4 == 0, (q - k) % 16 == 0, k <= q
    seen = [causal, k >= q, m4, m4 & causal, m16, m16 & causal, k < q]
    for i in range(QT):
        c = np.arange(CMP_PAD)[None, :]
        seen.append((c < CMP_N) & (c_end[None, :] <= q + i * P))
    masks = np.concatenate([np.where(m, 0.0, NEG) for m in seen], 1).astype(np.float32)
    import math
    li = [0.8 - 0.6 * math.exp(-0.3 * n) for n in range(LAYERS)]
    lam = np.array([[v, 1.0 - v] for v in li], np.float32)
    return dict(tables=tables, masks=masks, lam_inits=lam)


_INS = ("x norm1_g w_in q_norm_a k_norm_cmp k_norm_slc k_norm_win cmp_k_pos cmp_k_w1 cmp_k_w2 cmp_v_pos cmp_v_w1 "
        "cmp_v_w2 q_norm_b k_norm_b w_o_a w_o_b w_out norm2_g w_up w_down norm_attn_2 w_in_2 b_gate_2 diff_lambda_2 "
        "diff_subln_2 w_o_diff_2 w_o_sb_2 w_out_2 norm_ffn_2 w_ffn_in_2 w_ffn_out_2 norm_final_2").split()


def kernel(**inputs):
    import numpy as _np
    import concourse.bacc as _bacc
    from concourse.bass_utils import run_bass_kernel_spmd as _run

    nc = _bacc.Bacc("TRN2", target_bir_lowering=False, num_devices=1)
    arrays = {f"in_{n}": _np.ascontiguousarray(inputs[n]) for n in _INS}
    arrays.update({f"in_{n}": a for n, a in shape_tables().items()})
    aps = {n[3:]: nc.dram_tensor(n, a.shape, F32, kind="ExternalInput").ap() for n, a in arrays.items()}
    out = nc.dram_tensor("out", (1, S, D), F32, kind="ExternalOutput").ap()
    build(nc, aps, out)
    r = _run(nc, [arrays], core_ids=[0])
    return r.results[0]["out"]
```

```python
from contextlib import ExitStack

import concourse.bass as bass
from concourse import mybir

F32 = mybir.dt.float32
F32R = mybir.dt.float32r
BF16 = mybir.dt.bfloat16
ALU = mybir.AluOpType
ACT = mybir.ActivationFunctionType
AX_X = mybir.AxisListType.X

P = 128
S = 512
D = 1024
QT = S // P
KT = D // P
HD = 64
HALF = HD // 2
EPS = 1e-6
BANK = 512
NEG = -1e30
CMP_HEADS = 4
LAGS = dict(nsa=(4, 6), dil=(3, 5), diff=(4, 6), stick=(4, 6))
FF2 = 2816
LAYERS = 2
NSA_HEADS, NSA_GROUPS = 12, 3
CMP_N, CMP_PAD, CMP_STRIDE, CMP_LEN = 31, 32, 16, 32
CMP_HID = 256
CMP_COLS = S + 2 * CMP_STRIDE
CMP_ROWS = 2 * (CMP_COLS // CMP_STRIDE) + CMP_PAD
DIL_GROUPS, DIL_HPG = 3, 4
BLK = 4
RAW_RING, SPLIT_RING = 2, 3
BLK_COLS = BLK * BANK
GELU_A, GELU_B = 0.044715, 1.5957691216057308

CAUSAL, BAND, MOD4, MOD4C, MOD16, MOD16C, STRICT = range(7)
N_MASK = 7
(G_QA, G_KC, G_KS, G_KW, G_QB, G_KB) = range(6)

C_COS, C_SIN, C_COSC, C_SINC, C_VALID, C_ID = 0, 256, 512, 576, 640, 641
C_SPREAD = C_ID + P
C_ALL = C_SPREAD + 96
M_ALL = N_MASK * P + QT * CMP_PAD


class Block:

    def __init__(self, pieces, split=True):
        self.pieces, self.split = pieces, split
        self.kts = max(p[5] + p[2] for p in pieces)
        self.width = max(p[6] + p[4] for p in pieces)


class Panel:

    def __init__(self, blocks, width, kts=None, rope=None, turn=False, twice=False, query=False, dest=None, tile0=0,
                 col=0, src=None, up=False, group=0, tiles=0, split_at=None):
        self.blocks, self.width, self.kts = blocks, width, kts
        self.rope, self.turn, self.twice, self.query = rope, turn, twice, query
        self.dest, self.tile0, self.col, self.src = dest, tile0, col, src
        self.up, self.group, self.tiles, self.split_at = up, group, tiles, split_at


def panel(pieces, kts=KT, row=0, **what):
    blocks, k = [], 0
    while k < kts:
        n = min(BLK, kts - k)
        at, ps = 0, []
        for m, c, w in pieces:
            ps.append((m, row + k * P, n, c, w, 0, at))
            at += w
        blocks.append(Block(ps))
        k += n
    return Panel(blocks, at, kts=kts, **what)


def make_plan():
    w = "w_in"
    qa, kc, ks, vs, kw, vw, gn = 0, 768, 1152, 1344, 1536, 1728, 1920
    qb, kb, vb, gm = 1956, 2724, 3492, 4260
    first = [
        ("norm", [], dict(gain="norm1")),
        ("proj", [
            panel([(w, qa, 512)], rope=G_QA, dest="qa", tile0=0, query=True),
            panel([(w, vs, 192), (w, vw, 192), (w, gn, 36)], dest="nsa_v"),
            panel([(w, qa + 512, 256)], rope=G_QA, dest="qa", tile0=4, query=True),
            panel([(w, kc, 192)], turn=True, dest="cmp_in", tile0=0, twice=True),
            panel([(w, ks, 192)], rope=G_KS, dest="ks", tile0=0, twice=True),
            panel([(w, kw, 192)], rope=G_KW, dest="kw", tile0=0, twice=True),
            panel([(w, kc + 192, 192)], turn=True, dest="cmp_in", tile0=3, twice=True)], dict(who="nsa")),
        ("compress", [Panel([Block([(m, k * 8 * P, 8, 0, CMP_HID, 0, 0)], split=False)
                             for m in ("cmp_k_w1", "cmp_v_w1") for k in range(2)], CMP_HID)], {}),
        ("attend", [], dict(who="nsa")),
        ("turn", [], dict(src="y_nsa", tiles=6, tile0=0)),
        ("proj", [
            *[panel([(w, qb + 256 * n, 256)], rope=G_QB, dest="qb", tile0=2 * n, query=True) for n in range(3)],
            *[panel([(w, kb + 256 * n, 256)], rope=G_KB, dest="kb", tile0=2 * n) for n in range(3)],
            panel([(w, vb, 512)], dest="vb", col=0),
            panel([(w, vb + 512, 256)], dest="vb", col=512)], dict(who="dil")),
        ("attend", [], dict(who="dil")),
        ("turn", [], dict(src="y_dil", tiles=2, tile0=6)),
        ("gates", [panel([(w, gm + 512 * n, 512)]) for n in range(4)], dict(bias=False)),
        ("mix", [Panel([Block([("w_o_a", 0, 4, 256 * n, 256, 0, 0)]),
                        Block([("w_o_a", 4 * P, 2, 256 * n, 256, 0, 0), ("w_o_b", 0, 2, 256 * n, 256, 2, 0)])],
                       256, split_at=6) for n in range(4)], {}),
        ("add", [panel([("w_out", 512 * n, 512)], src="h", col=512 * n) for n in range(2)], {}),
        ("norm", [], dict(gain="norm2")),
        ("ffn", [], dict(gated=False, groups=[8] * 4)),
    ]
    w = "w_in_2"
    layer = [
        ("norm", [], dict(gain="norm_attn")),
        ("proj", [
            panel([(w, 0, 512)], rope=-1, dest="dq", tile0=0, query=True),
            panel([(w, 512, 512)], rope=-1, dest="dk", tile0=0),
            panel([(w, 1024, 512)], dest="dv", col=0)], dict(who="diff")),
        ("attend", [], dict(who="diff")),
        ("subln", [], {}),
        ("turn", [], dict(src="y_diff", tiles=4, tile0=0, gain="subln")),
        ("proj", [
            panel([(w, 1536, 512)], turn=True, dest="dq", tile0=0, query=True),
            panel([(w, 2048, 512)], turn=True, dest="dk", tile0=0),
            panel([(w, 2560, 512)], dest="dv", col=0)], dict(who="stick")),
        ("attend", [], dict(who="stick")),
        ("turn", [], dict(src="y_diff", tiles=4, tile0=4)),
        ("gates", [panel([(w, 3072 + 512 * n, 512)]) for n in range(4)], dict(bias=True)),
        ("mix", [Panel([Block([("w_o_diff_2", 0, 4, 256 * n, 256, 0, 0)]),
                        Block([("w_o_sb_2", 0, 4, 256 * n, 256, 0, 0)])], 256, split_at=4) for n in range(4)], {}),
        ("add", [panel([("w_out_2", 512 * n, 512)], src="h", col=512 * n) for n in range(2)], {}),
        ("norm", [], dict(gain="norm_ffn")),
        ("ffn", [], dict(gated=True, groups=[8, 8, 6])),
    ]
    for kind, panels, how in first + layer:
        if kind != "ffn":
            continue
        row = 0
        for g, kts in enumerate(how["groups"]):
            per = 2 if how["gated"] else 4
            for t in range(0, kts, per):
                c = (row + t) * P
                ps = [("w_ffn_in_2", c, 256), ("w_ffn_in_2", FF2 + c, 256)] if how["gated"] else [("w_up", c, 512)]
                panels.append(panel(ps, up=True, tile0=t, group=g, tiles=per))
            for n in range(2):
                m = "w_ffn_out_2" if how["gated"] else "w_down"
                panels.append(panel([(m, 512 * n, 512)], kts=kts, row=row * P, src="mid", col=512 * n, group=g))
            row += kts
    return first, layer


def attention_units(who):
    units, sets = [], 0
    for i in range(QT):
        w = (i + 1) * P
        diag = [(i * P, CAUSAL)]
        if who == "nsa":
            for h0 in range(0, NSA_HEADS, CMP_HEADS):
                units.append(dict(i=i, h=h0, br=0, set=sets, slot=0, size=CMP_HEADS, vd=HD, head0=h0, cmp=True,
                                  width=P, j0=0, nj=1))
                sets += 1
            for h0 in range(0, NSA_HEADS, 4):
                for br in range(2):
                    for hh in range(4):
                        units.append(dict(i=i, h=h0 + hh, br=br, set=sets, slot=br * 4 + hh, size=8, vd=HD, head0=h0,
                                          width=w, j0=0, nj=i + 1, masks=diag))
                sets += 1
        if who == "dil":
            for h0 in range(0, DIL_HPG, 2):
                for g in range(DIL_GROUPS):
                    for hh in range(2):
                        j0 = max(0, i - 1) if g == 0 else 0
                        off, own = ((BAND, CAUSAL), (MOD4, MOD4C), (MOD16, MOD16C))[g]
                        units.append(dict(i=i, h=g * DIL_HPG + h0 + hh, br=g, set=sets, slot=g * 2 + hh, size=6, vd=HD,
                                          head0=h0, width=(i + 1 - j0) * P, j0=j0, nj=i + 1 - j0,
                                          masks=[((j - j0) * P, own if j == i else off) for j in range(j0, i + 1)]))
                sets += 1
        if who == "diff":
            for h0 in range(0, 4, 2):
                for hh in range(2):
                    for c in range(2):
                        units.append(dict(i=i, h=(h0 + hh) * 2 + c, br=c, set=sets, slot=hh * 2 + c, size=4, vd=P,
                                          head0=h0, width=w, j0=0, nj=i + 1, masks=diag))
                sets += 1
        if who == "stick":
            for h in range(8):
                units.append(dict(i=i, h=h, br=0, set=sets, slot=h, size=8, vd=HD, head0=0,
                                  width=w, j0=0, nj=i + 1, masks=[(i * P, STRICT)]))
            sets += 1
    sizes = [0] * sets
    for u in units:
        u.setdefault("cmp", False)
        sizes[u["set"]] = 0 if u["cmp"] else 1
    plain = [o for o in range(sets) if sizes[o]]
    for s, u in enumerate(units):
        n = plain.index(u["set"]) if not u["cmp"] else 0
        u["place"], u["before_set"] = n % 4, n
        u["before"] = plain[n - 4] if n >= 4 else None
        u["ends_set"] = s == len(units) - 1 or units[s + 1]["set"] != u["set"]
    return units, sets


def build(nc, A, out):
    first, layer = make_plan()
    stages = first + layer

    blocks, n_split, n_direct = [], 0, 0
    layer_block0 = None
    for n, (kind, panels, how) in enumerate(stages):
        how["follows"] = stages[n - 1][0] if n else None
        if n == len(first):
            layer_block0 = len(blocks)
        for p in panels:
            for b in p.blocks:
                b.raw = len(blocks)
                b.spl, b.direct = n_split, n_direct
                if b.split:
                    n_split += 1
                else:
                    n_direct += 1
                blocks.append(b)
        last = n == len(first) - 1 or n == len(stages) - 1 or stages[n + 1][0] == "compress"
        before_norm = not last and stages[n + 1][0] == "norm"
        before_attend = not last and stages[n + 1][0] == "attend"
        how["spl_ahead"] = n_split + (0 if last else SPLIT_RING - 1 if before_norm or before_attend else SPLIT_RING)
    per_layer_blocks = len(blocks) - layer_block0
    assert per_layer_blocks % (RAW_RING * SPLIT_RING) == 0 and len(first) > 0

    def adds(stage):
        kind, panels, how = stage
        a = dict(stage_end=4)
        if kind == "norm":
            a.update(squares=QT, mean=QT, root=QT, scaled=QT, turned_ps=KT, split_hi=KT, split_lo=KT)
        if kind == "turn":
            a.update(turned_ps=how["tiles"], split_hi=how["tiles"], split_lo=how["tiles"])
        if kind == "proj":
            ropes = [p for p in panels if p.rope is not None]
            turns = [p for p in panels if p.rope is not None or p.turn]
            tiles = sum(turn_tiles(p) for p in turns)
            normed = [p for p in ropes if p.rope >= 0]
            a.update(staged=QT * len(panels), squares=len(normed), mean=len(normed), root=len(normed),
                     scaled=len(ropes), crossed=len(ropes), roped=len(ropes), turned_ps=tiles, turned=tiles)
        if kind == "compress":
            a.update(direct_used=4, pre_ps=2, pre=2, hidden_ps=2, hidden=2, gate_arg=2, gate_sig=2, cmp_ps=2, cmp_v=1, mean=1, root=1,
                     roped=1, turned_ps=1, turned=1)
        if kind == "attend":
            units, sets = attention_units(how["who"])
            n = len(units)
            a.update(scores=n, probs=n, probs_turned=n, pT_act=n // 2, pT_dve=n // 2, outs=n, combined=sets)
            if how["who"] == "stick":
                a.update(stick_scan=n, stick_weights=n)
            else:
                a.update(negmax=n)
            if how["who"] == "nsa":
                a.update(cmp_den=3 * QT, summed=3 * QT)
            if how["who"] == "dil":
                a.update(lse_gap=sets, lse_exp=sets)
            if how["who"] == "diff":
                a.update(lam_dots=1, lam_exps=1)
        if kind == "subln":
            a.update(mean=1, root=1, roped=1)
        if kind == "gates":
            a.update(gated=16)
        if kind == "mix":
            a.update(parts=8, mixed=8, split_hi=8, split_lo=8)
        if kind == "add":
            a.update(added=QT * len(panels))
        if kind == "ffn":
            ups = sum(p.tiles for p in panels if p.up)
            downs = len([p for p in panels if not p.up])
            a.update(acted=ups, mixed=ups, split_hi=ups, split_lo=ups, added=QT * downs)
        spl = sum(b.split for p in panels for b in p.blocks)
        a.update(split_blocks=spl)
        return a

    def turn_tiles(p):
        return p.width // HD if p.twice else p.width // P

    total, per_layer = {}, {}
    for n, st in enumerate(stages):
        st[2]["base"] = dict(total)
        for k, v in adds(st).items():
            total[k] = total.get(k, 0) + v
            if n >= len(first):
                per_layer[k] = per_layer.get(k, 0) + v

    def value(st, name, n, loop):
        v = st[2]["base"].get(name, 0) + n
        return v if loop is None else v + loop * per_layer[name]

    with ExitStack() as ctx:
        def sb(name, shape, dt=F32, scope=ctx):
            return scope.enter_context(nc.sbuf_tensor(name, shape, dt))

        def sem(name):
            return ctx.enter_context(nc.semaphore(name))

        x_sb = sb("x_sb", [P, QT, D])
        h_hi, h_lo = sb("h_hi", [P, KT, S], F32R), sb("h_lo", [P, KT, S], F32R)
        raw = sb("raw", [P, RAW_RING, BLK_COLS])
        w_hi = sb("w_hi", [P, SPLIT_RING, BLK_COLS], F32R)
        w_lo = sb("w_lo", [P, SPLIT_RING, BLK_COLS], F32R)
        tables = sb("tables", [P, C_ALL])
        masks = sb("masks", [P, M_ALL], BF16)
        ident_b = sb("ident_b", [P, P], BF16)
        gains = sb("gains", [P, 6, HD])
        gcos, gsin = sb("gcos", [P, QT, HD]), sb("gsin", [P, QT, HD])
        small = sb("small", [P, 192])
        gcol = sb("gcol", [P, 4, KT])
        bgate = sb("bgate", [P, 2 * KT])
        sub_col = sb("sub_col", [P, 4])
        pos_col = sb("pos_col", [P, 2, 16])
        w2_sb = sb("w2_sb", [P, 2, 2, HD])
        lam_in = sb("lam_in", [P, 4 * HD])
        lam_init = sb("lam_init", [P, 2])
        negmax_t = sb("negmax_t", [P, 4, 8])
        den_t = sb("den_t", [P, 4, 8])
        ident = tables[:, C_ID:C_ID + P]

        def four(t):
            return [t[:, n, :] for n in range(4)]

        with ExitStack() as r:
            m_hi, m_lo = sb("m_hi", [P, KT, S], F32R, r), sb("m_lo", [P, KT, S], F32R, r)
        with ExitStack() as r:
            stage_s, stage_t = sb("stage_s", [P, QT, BANK], F32, r), sb("stage_t", [P, QT, BANK], F32, r)
            stage_u = sb("stage_u", [P, QT, BANK], F32, r)
        with ExitStack() as r:
            cmp_pre = sb("cmp_pre", [P, 2, CMP_HID], F32, r)
        with ExitStack() as r:
            nsa_bufs = (sb("nsa_probs", [P, 4, BANK], F32, r), four(sb("nsa_pT", [P, 4, BANK], F32, r)),
                        sb("nsa_parts", [P, 512], F32, r))
            cmp_x = sb("cmp_x", [P, NSA_GROUPS, P], F32, r)
        with ExitStack() as r:
            sb("m_hi_six", [P, 6, S], F32, r)
            dil_pT = sb("dil_pT", [P, 2, BANK], F32, r)
            sb("m_lo_six", [P, 6, S], F32, r)
            dil_pT2 = sb("dil_pT2", [P, 2, BANK], F32, r)
        with ExitStack() as r:
            sb("m_hi_first", [P, 4, S], F32, r)
            stick_rem = sb("stick_rem", [P, 2, BANK], F32, r)
            stick_after = sb("stick_after", [P, 2, BANK], F32, r)
        sb("mid_space", [P, 2 * KT * S])

        dest = {}
        with ExitStack() as r:
            dest["qa"], dest["ks"], dest["kw"] = (sb("q_nsa", [P, 6, S], F32, r), sb("k_slc", [P, 3, S], F32, r),
                                                  sb("k_win", [P, 3, S], F32, r))
            v_nsa, g_nsa = sb("v_nsa", [P, QT, 384], F32, r), sb("g_nsa", [P, QT, 36], F32, r)
            kc_T, vc = sb("kc_T", [P, 3, 2, CMP_PAD], F32, r), sb("vc", [P, 3, CMP_HEADS, HD], F32, r)
            with ExitStack() as r2:
                cmp_in = sb("cmp_in", [P, 6, CMP_COLS], F32, r2)
                hid_z, hid_s, hid_h = (sb("hid_z", [P, 192], F32, r2), sb("hid_s", [P, 192], F32, r2),
                                       sb("hid_h", [P, 2, 192], F32, r2))
                kc_n, kc_t = sb("kc_n", [P, HD], F32, r2), sb("kc_t", [P, HD], F32, r2)
                kc_u = sb("kc_u", [P, 2 * HD], F32, r2)
            with ExitStack() as r2:
                y_nsa = sb("y_nsa", [P, QT, 768], F32, r2)
        with ExitStack() as r:
            dest["qb"], dest["kb"] = sb("q_dil", [P, 6, S], F32, r), sb("k_dil", [P, 6, S], F32, r)
            v_dil = sb("v_dil", [P, QT, 768], F32, r)
            with ExitStack() as r2:
                stage_dil = tuple(sb(f"stage_dil_{n}", [P, QT, 256], F32, r2) for n in "stu")
            with ExitStack() as r2:
                dil_bufs = (sb("dil_probs", [P, 4, BANK], F32, r2),
                            [dil_pT[:, 0, :], dil_pT[:, 1, :], dil_pT2[:, 0, :], dil_pT2[:, 1, :]],
                            sb("dil_parts", [P, 512], F32, r2))
                y_dil = sb("y_dil", [P, QT, 256], F32, r2)
        with ExitStack() as r:
            dest["dq"], dest["dk"] = sb("q_two", [P, 4, S], F32, r), sb("k_two", [P, 4, S], F32, r)
            v_two = sb("v_two", [P, QT, 512], F32, r)
            two_bufs = (sb("two_probs", [P, 4, BANK], F32, r), four(sb("two_pT", [P, 4, BANK], F32, r)),
                        sb("two_parts", [P, 512], F32, r))
            y_two = sb("y_two", [P, QT, 512], F32, r)
            stage_two = two_bufs[0]
        with ExitStack() as r:
            gate_T = sb("gate_T", [P, 16, S], F32, r)
            part_a, part_b = sb("part_a", [P, 2, S], F32, r), sb("part_b", [P, 2, S], F32, r)
        with ExitStack() as r:
            act_out, hid_m = sb("act_out", [P, 2, S], F32, r), sb("hid_m", [P, 2, S], F32, r)
            square_junk, root_diag = sb("square_junk", [P, D], F32, r), sb("root_diag", [P, QT, P], F32, r)
            g_final, out_sb = sb("g_final", [P, D], F32, r), sb("out_sb", [P, QT, D], F32, r)
        with ExitStack() as r:
            mask_f = sb("mask_f", [P, M_ALL], F32, r)

        ps = [ctx.enter_context(nc.psum_tensor(f"bank{b}", [P, BANK], F32)) for b in range(8)]

        x_in = [sem(f"x_in{i}") for i in range(QT)]
        consts_in, more_in, gain_in, col_in = sem("consts_in"), sem("more_in"), sem("gain_in"), sem("col_in")
        landed = [sem(f"landed{i}") for i in range(RAW_RING)]
        w_hi_ready, w_lo_ready, products, direct_used = (sem("w_hi_ready"), sem("w_lo_ready"), sem("products"),
                                                         sem("direct_used"))
        stage_end = sem("stage_end")
        names = ("squares mean root scaled turned_ps turned split_hi split_lo staged crossed roped hidden_ps hidden "
                 "gate_arg gate_sig summed cmp_ps cmp_v pre_ps pre scores probs probs_turned pT_act pT_dve outs combined "
                 "stick_scan stick_weights negmax lse_gap lse_exp lam_dots lam_exps gated parts mixed added "
                 "acted out_ready cmp_den").split()
        sm = {n: sem(n) for n in names}
        sm["stage_end"] = stage_end
        sm["direct_used"] = direct_used
        stored, final_in = sem("stored"), sem("final_in")
        block = ctx.enter_context(nc.Block())

        def staging(st):
            return dict(nsa=(stage_s, stage_t, stage_u), dil=stage_dil, diff=(stage_s, stage_t, stage_u),
                        stick=(None, None, stage_two))[st[2]["who"]]

        def of_blocks(n, scale, loop):
            return n * scale if loop is None else n * scale + loop * (per_layer_blocks * scale)

        def view(ring, slot, b):
            return ring[:, slot, 0:b.kts * b.width].rearrange("p (k n) -> p k n", k=b.kts)

        def raw_direct(b):
            return raw[:, b.raw % RAW_RING, :].rearrange("p (k n) -> p k n", k=8)

        landed_at = {}
        counts = [0] * RAW_RING
        for b in blocks:
            counts[b.raw % RAW_RING] += 16 * len(b.pieces)
            landed_at[b.raw] = counts[b.raw % RAW_RING]
        layer_landed = [sum(16 * len(b.pieces) for b in blocks[layer_block0:] if b.raw % RAW_RING == i)
                        for i in range(RAW_RING)]

        def landing(b, loop):
            return landed_at[b.raw] if loop is None else landed_at[b.raw] + loop * layer_landed[b.raw % RAW_RING]

        split_list = [b for b in blocks if b.split]

        class Splitter:

            def __init__(self, eng, which):
                self.eng, self.which, self.next = eng, which, 0

            def upto(self, st, n, loop):
                while self.next < min(n, st[2]["spl_ahead"]):
                    b = split_list[self.next]
                    slot = b.spl % SPLIT_RING
                    n_el = b.kts * b.width
                    if self.which == "hi":
                        self.eng.wait_ge(landed[b.raw % RAW_RING], landing(b, loop))
                        if b.spl >= SPLIT_RING:
                            self.eng.wait_ge(products, of_blocks(b.spl - SPLIT_RING + 1, 4, loop))
                        nc.scalar.activation(w_hi[:, slot, 0:n_el], raw[:, b.raw % RAW_RING, 0:n_el],
                                             ACT.Copy).then_inc(w_hi_ready, 1)
                    else:
                        self.eng.wait_ge(w_hi_ready, of_blocks(b.spl + 1, 1, loop))
                        nc.vector.tensor_tensor(w_lo[:, slot, 0:n_el], raw[:, b.raw % RAW_RING, 0:n_el],
                                                w_hi[:, slot, 0:n_el].bitcast(F32),
                                                ALU.subtract).then_inc(w_lo_ready, 1)
                    self.next += 1

        def last_block(p):
            return p.blocks[-1].spl

        def bank_count(p, q, loop):
            n = 4 * last_block(p) + q + 1
            return n if loop is None else n + loop * (4 * per_layer_blocks)

        def bank_set(k):
            return 4 * (k % 2)

        CONST_LOADS, MORE_LOADS, LAYER_LOADS = 2, 12, 5

        def gain_col(st):
            return gcol[:, dict(norm1=0, norm2=1, norm_attn=2, norm_ffn=3)[st[2]["gain"]], :]

        def turn_gain(st):
            return (lambda t: sub_col[:, 1:2]) if st[2].get("gain") == "subln" else None

        def bufs(who):
            return dict(nsa=nsa_bufs, dil=dil_bufs, diff=two_bufs, stick=two_bufs)[who]

        def evac(eng, st, loop, units, t, pT, copy, args, name):
            u = units[t]
            eng.wait_ge(sm["probs_turned"], value(st, "probs_turned", t + 1, loop))
            if t >= 4:
                eng.wait_ge(sm["outs"], value(st, "outs", t - 3, loop))
            n = slice(0, u["nj"] * P)
            copy(pT[t % 4][:, n], ps[4 + t % 2][:, n], *args).then_inc(sm[name], 1)

        @block.sync
        def _(sp):
            for i in range(QT):
                sp.dma_start(x_sb[:, i, :], A["x"][0, i * P:(i + 1) * P, :]).then_inc(x_in[i], 16)

            def loads(bs, loop):
                for b in bs:
                    prev = blocks[b.raw - RAW_RING] if b.raw >= RAW_RING else None
                    if prev is not None and prev.split:
                        sp.wait_ge(w_lo_ready, of_blocks(prev.spl + 1, 1, loop))
                    elif prev is not None:
                        sp.wait_ge(direct_used, prev.direct + 1)
                    dst = raw[:, b.raw % RAW_RING, 0:b.kts * b.width].rearrange("p (k n) -> p k n", k=b.kts)
                    for m, r0, kts, c0, n, k_at, c_at in b.pieces:
                        w = A[m][0] if loop is None else A[m][bass.ds(loop, 1)].rearrange("a r c -> (a r) c")
                        sp.dma_start(dst[:, k_at:k_at + kts, c_at:c_at + n],
                                     w[r0:r0 + kts * P, c0:c0 + n].rearrange("(k p) n -> p k n", p=P)
                                     ).then_inc(landed[b.raw % RAW_RING], 16)

            loads(blocks[:layer_block0], None)
            with sp.Fori(0, LAYERS) as loop:
                loads(blocks[layer_block0:], loop)
            sp.wait_ge(stored, 16 * QT)

        @block.scalar
        def _(act):
            spl = Splitter(act, "hi")

            def norm(st, loop):
                if st is layer[0]:
                    spl.upto(st, st[2]["spl_ahead"] - 1, loop)
                for i in range(QT + 1):
                    if i < QT:
                        if st is first[0]:
                            act.wait_ge(x_in[i], 16)
                        else:
                            act.wait_ge(sm["added"], value(st, "added", i + 1 - QT, loop))
                        if i:
                            act.wait_ge(sm["squares"], value(st, "squares", i, loop))
                        nc.scalar.activation(square_junk[:, :], x_sb[:, i, :], ACT.Square,
                                             accum_out=small[:, i:i + 1]).then_inc(sm["squares"], 1)
                    if i:
                        act.wait_ge(sm["mean"], value(st, "mean", i, loop))
                        nc.scalar.activation(small[:, 3 + i:4 + i], small[:, 3 + i:4 + i],
                                             ACT.Sqrt).then_inc(sm["root"], 1)
                if st is first[0]:
                    spl.upto(st, 1, loop)
                if st is first[0]:
                    act.wait_ge(consts_in, CONST_LOADS * 16)
                if st is layer[0]:
                    act.wait_ge(gain_in, loop * 16 + 16)

            def turn(st, loop, hi, tiles, tile0, gain):
                for t in range(tiles):
                    act.wait_ge(sm["turned_ps"], value(st, "turned_ps", t + 1, loop))
                    nc.scalar.activation(hi[:, tile0 + t, :], ps[t % 8][:, :], ACT.Copy,
                                         scale=1.0 if gain is None else gain(t)).then_inc(sm["split_hi"], 1)

            def proj(st, loop):
                stage_s, stage_t, stage_u = staging(st)
                panels = st[1]
                staged, tp, n_root, n_roped = 0, 0, 0, 0
                pending = None

                def finish(p, tp):
                    for c in range(turn_tiles(p)):
                        act.wait_ge(sm["turned_ps"], value(st, "turned_ps", tp + c + 1, loop))
                        b = ps[p.set + c % 4]
                        if p.dest == "cmp_in":
                            c += p.tile0
                            nc.scalar.activation(cmp_in[0:HD, c, 0:S], b[0:HD, :], ACT.Copy)
                            nc.scalar.activation(cmp_in[HD:P, c, 0:S - 1], b[HD:P, 1:S],
                                                 ACT.Copy).then_inc(sm["turned"], 1)
                        else:
                            nc.scalar.activation(dest[p.dest][:, p.tile0 + c, :], b[:, :],
                                                 ACT.Copy).then_inc(sm["turned"], 1)
                    return tp + turn_tiles(p)

                for k, p in enumerate(panels):
                    p.set = bank_set(k)
                    spl.upto(st, last_block(p) + SPLIT_RING, loop)
                    roped = p.rope is not None
                    if roped and n_roped:
                        act.wait_ge(sm["roped"], value(st, "roped", n_roped, loop))
                    if p.turn and pending is not None:
                        tp = finish(pending, tp)
                        pending = None
                    for i in range(QT):
                        act.wait_ge(products, bank_count(p, i, loop))
                        b = ps[p.set + i]
                        if p.dest == "nsa_v":
                            nc.scalar.activation(v_nsa[:, i, :], b[:, 0:384], ACT.Copy)
                            ins = nc.scalar.activation(g_nsa[:, i, :], b[:, 384:420], ACT.Sigmoid)
                        elif p.dest in ("vb", "dv"):
                            to = v_dil if p.dest == "vb" else v_two
                            ins = nc.scalar.activation(to[:, i, p.col:p.col + p.width], b[:, 0:p.width], ACT.Copy)
                        elif p.twice and not roped:
                            heads = b[:, 0:p.width].rearrange("p (h d) -> p h d", d=HD)
                            pair = stage_u[:, i, 0:2 * p.width].rearrange("p (h c d) -> p h c d", c=2, d=HD)
                            nc.scalar.activation(pair[:, :, 0, :], heads, ACT.Copy)
                            ins = nc.scalar.activation(pair[:, :, 1, :], heads, ACT.Copy)
                        else:
                            to = stage_s if roped else stage_u
                            scale = HD ** -0.5 if p.query and not (roped and p.rope >= 0) else 1.0
                            ins = nc.scalar.activation(to[:, i, 0:p.width], b[:, 0:p.width], ACT.Copy, scale=scale)
                        ins.then_inc(sm["staged"], 1)
                    if pending is not None:
                        tp = finish(pending, tp)
                        pending = None
                    if roped:
                        n_roped += 1
                        if p.rope >= 0:
                            n_root += 1
                            act.wait_ge(sm["mean"], value(st, "mean", n_root, loop))
                            n = QT * p.width // HD
                            nc.scalar.activation(small[:, 32:32 + n], small[:, 0:n], ACT.Sqrt).then_inc(sm["root"], 1)
                    if roped or p.turn:
                        pending = p
                if pending is not None:
                    finish(pending, tp)

            def compress(st, loop):
                for kv in range(2):
                    act.wait_ge(sm["pre_ps"], value(st, "pre_ps", kv + 1, loop))
                    nc.scalar.activation(cmp_pre[0:CMP_ROWS, kv, :], ps[kv][0:CMP_ROWS, 0:CMP_HID],
                                         ACT.Copy).then_inc(sm["pre"], 1)
                    act.wait_ge(sm["gate_arg"], value(st, "gate_arg", kv + 1, loop))
                    nc.scalar.activation(hid_s[:, :], hid_s[:, :], ACT.Sigmoid).then_inc(sm["gate_sig"], 1)
                    if kv == 0:
                        act.wait_ge(sm["mean"], value(st, "mean", 1, loop))
                        nc.scalar.activation(small[0:96, 1:2], small[0:96, 1:2], ACT.Sqrt).then_inc(sm["root"], 1)
                act.wait_ge(sm["turned_ps"], value(st, "turned_ps", 1, loop))
                for n in range(2):
                    r = slice(n * HD, (n + 1) * HD)
                    ins = nc.scalar.activation(kc_T[r, :, n, :],
                                               ps[6][r, 0:96].rearrange("p (g c) -> p g c", g=3), ACT.Copy)
                ins.then_inc(sm["turned"], 1)
                act.wait_ge(sm["cmp_ps"], value(st, "cmp_ps", 2, loop))
                for n in range(CMP_HEADS):
                    r = slice(n * CMP_PAD, (n + 1) * CMP_PAD)
                    ins = nc.scalar.activation(vc[r, :, n, :], ps[5][r, 0:192].rearrange("p (g d) -> p g d", g=3),
                                               ACT.Copy)
                ins.then_inc(sm["cmp_v"], 1)

            def attend(st, loop):
                who = st[2]["who"]
                lag_turn, lag_out = LAGS[who]
                units, sets = attention_units(who)
                probs, pT, parts = bufs(who)
                if who == "diff":
                    act.wait_ge(col_in, loop * (16 * LAYER_LOADS) + 16 * LAYER_LOADS)
                    act.wait_ge(sm["lam_dots"], value(st, "lam_dots", 1, loop))
                    nc.scalar.activation(small[:, 2:4], small[:, 0:2], ACT.Exp).then_inc(sm["lam_exps"], 1)
                for s in range(len(units) + lag_out):
                    if s < len(units):
                        u = units[s]
                        W, o = u["width"], u["set"]
                        src = ps[s % 4][:, 0:W]
                        if s >= 4:
                            act.wait_ge(sm["probs_turned"], value(st, "probs_turned", s - 3, loop))
                        if who == "stick":
                            if s >= 2:
                                act.wait_ge(sm["stick_scan"], value(st, "stick_scan", s - 1, loop))
                            act.wait_ge(sm["scores"], value(st, "scores", s + 1, loop))
                            nc.scalar.activation(probs[:, s % 4, 0:W], src, ACT.Sigmoid)
                            nc.scalar.activation(stick_rem[:, s % 2, 0:W], src, ACT.Sigmoid,
                                                 scale=-1.0).then_inc(sm["probs"], 1)
                        elif u["cmp"]:
                            act.wait_ge(sm["negmax"], value(st, "negmax", s + 1, loop))
                            nc.scalar.activation(probs[:, s % 4, 0:W], cmp_x[:, u["h"] // CMP_HEADS, :],
                                                 ACT.Exp).then_inc(sm["probs"], 1)
                        else:
                            if u["slot"] == 0 and u["before"] is not None:
                                act.wait_ge(sm["combined"], value(st, "combined", u["before"] + 1, loop))
                            act.wait_ge(sm["negmax"], value(st, "negmax", s + 1, loop))
                            nc.scalar.activation(probs[:, s % 4, 0:W], src, ACT.Exp,
                                                 bias=negmax_t[:, u["place"], u["slot"]:u["slot"] + 1],
                                                 accum_out=den_t[:, u["place"], u["slot"]:u["slot"] + 1]
                                                 ).then_inc(sm["probs"], 1)
                    t = s - lag_turn
                    if 0 <= t < len(units) and t % 2 == 0:
                        evac(act, st, loop, units, t, pT, nc.scalar.activation, (ACT.Copy,), "pT_act")
                    if who == "dil" and s >= 2 and s - 2 < len(units) and units[s - 2]["ends_set"]:
                        o = units[s - 2]["set"]
                        act.wait_ge(sm["lse_gap"], value(st, "lse_gap", o + 1, loop))
                        nc.scalar.activation(small[:, 0:6], small[:, 0:6], ACT.Exp).then_inc(sm["lse_exp"], 1)

            def subln(st, loop):
                act.wait_ge(sm["mean"], value(st, "mean", 1, loop))
                nc.scalar.activation(small[:, 16:32], small[:, 16:32], ACT.Sqrt).then_inc(sm["root"], 1)

            def gates(st, loop):
                for k, p in enumerate(st[1]):
                    spl.upto(st, last_block(p) + SPLIT_RING, loop)
                    for q in range(4):
                        act.wait_ge(products, bank_count(p, q, loop))
                        t = 4 * k + q
                        nc.scalar.activation(gate_T[:, t, :], ps[bank_set(k) + q][:, :], ACT.Sigmoid,
                                             bias=bgate[:, t:t + 1] if st[2]["bias"] else 0.0
                                             ).then_inc(sm["gated"], 1)

            def mix(st, loop):
                for k, p in enumerate(st[1]):
                    spl.upto(st, last_block(p) + SPLIT_RING, loop)
                    for q in range(2):
                        t = 2 * k + q
                        act.wait_ge(sm["mixed"], value(st, "mixed", t + 1, loop))
                        nc.scalar.activation(h_hi[:, t, :], part_a[:, t % 2, :],
                                             ACT.Copy).then_inc(sm["split_hi"], 1)

            def add(st, loop):
                for p in st[1]:
                    spl.upto(st, last_block(p) + SPLIT_RING, loop)

            def ffn(st, loop):
                gated = st[2]["gated"]
                m = 0
                for k, p in enumerate(st[1]):
                    spl.upto(st, last_block(p) + SPLIT_RING, loop)
                    if not p.up:
                        continue
                    for q in range(p.tiles + 1):
                        if q < p.tiles:
                            t = m + q
                            if t >= 2:
                                act.wait_ge(sm["mixed"], value(st, "mixed", t - 1, loop))
                            act.wait_ge(products, bank_count(p, q, loop))
                            nc.scalar.activation(act_out[:, t % 2, :], ps[bank_set(k) + q][:, :],
                                                 ACT.Sigmoid if gated else ACT.Relu).then_inc(sm["acted"], 1)
                        if q >= 1:
                            t = m + q - 1
                            act.wait_ge(sm["mixed"], value(st, "mixed", t + 1, loop))
                            nc.scalar.activation(m_hi[:, p.tile0 + q - 1, :], hid_m[:, t % 2, :],
                                                 ACT.Copy).then_inc(sm["split_hi"], 1)
                    m += p.tiles

            def stage(st, loop):
                kind = st[0]
                if kind == "norm":
                    norm(st, loop)
                    turn(st, loop, h_hi, KT, 0, lambda t: gain_col(st)[:, t:t + 1])
                elif kind == "turn":
                    turn(st, loop, m_hi, st[2]["tiles"], st[2]["tile0"], turn_gain(st))
                else:
                    dict(proj=proj, compress=compress, attend=attend, subln=subln, gates=gates, mix=mix, add=add,
                         ffn=ffn)[kind](st, loop)
                act.drain().then_inc(stage_end, 1)
                spl.upto(st, st[2]["spl_ahead"], loop)
                if kind not in ("add", "ffn"):
                    act.wait_ge(sm["stage_end"], value(st, "stage_end", 4, loop))

            act.dma_start(tables[:, :], A["tables"]).then_inc(consts_in, 16)
            act.dma_start(gcol[:, 0, :], A["norm1_g"][0].rearrange("(k p) -> p k", p=P),
                          allow_slow_non_contiguous=True).then_inc(consts_in, 16)
            for st in first:
                stage(st, None)
            with act.Fori(0, LAYERS) as loop:
                for st in layer:
                    stage(st, loop)
            for i in range(QT + 1):
                if i < QT:
                    act.wait_ge(sm["added"], total["added"] + per_layer["added"] + i + 1 - QT)
                    if i:
                        act.wait_ge(sm["squares"], total["squares"] + per_layer["squares"] + i)
                    nc.scalar.activation(square_junk[:, :], x_sb[:, i, :], ACT.Square,
                                         accum_out=small[:, i:i + 1]).then_inc(sm["squares"], 1)
                if i:
                    act.wait_ge(sm["mean"], total["mean"] + per_layer["mean"] + i)
                    nc.scalar.activation(small[:, 3 + i:4 + i], small[:, 3 + i:4 + i], ACT.Sqrt).then_inc(sm["root"], 1)
            for i in range(QT):
                act.wait_ge(sm["out_ready"], i + 1)
                act.dma_start(out[0, i * P:(i + 1) * P, :], out_sb[:, i, :]).then_inc(stored, 16)

        @block.gpsimd
        def _(pool):
            def proj(st, loop):
                stage_s, stage_t, stage_u = staging(st)
                n_sq = n_rope = staged = 0
                for k, p in enumerate(st[1]):
                    staged += QT
                    if p.rope is None:
                        continue
                    s4 = stage_s[:, :, 0:p.width].rearrange("p i (h d) -> p i h d", d=HD)
                    t4 = stage_t[:, :, 0:p.width].rearrange("p i (h d) -> p i h d", d=HD)
                    if n_rope:
                        pool.wait_ge(sm["roped"], value(st, "roped", n_rope, loop))
                    pool.wait_ge(sm["staged"], value(st, "staged", staged, loop))
                    if p.rope >= 0:
                        n_sq += 1
                        nc.gpsimd.tensor_tensor(stage_t[:, :, 0:p.width], stage_s[:, :, 0:p.width],
                                                stage_s[:, :, 0:p.width], ALU.mult).then_inc(sm["squares"], 1)
                    n_rope += 1
                    pool.wait_ge(sm["scaled"], value(st, "scaled", n_rope, loop))
                    nh = p.width // HD
                    shape = [P, QT, nh, HALF]
                    nc.gpsimd.tensor_tensor(t4[:, :, :, 0:HALF], s4[:, :, :, HALF:HD],
                                            gsin[:, :, 0:HALF].unsqueeze(2).to_broadcast(shape), ALU.mult)
                    nc.gpsimd.tensor_tensor(t4[:, :, :, HALF:HD], s4[:, :, :, 0:HALF],
                                            gsin[:, :, HALF:HD].unsqueeze(2).to_broadcast(shape),
                                            ALU.mult).then_inc(sm["crossed"], 1)

            def attend_nsa(st, loop):
                parts, n = bufs("nsa")[2], 0
                for u in attention_units("nsa")[0]:
                    if u["cmp"] or not u["ends_set"]:
                        continue
                    n += 1
                    pool.wait_ge(sm["combined"], value(st, "combined", u["set"] + 1, loop))
                    y = y_nsa[:, u["i"], u["head0"] * HD:(u["head0"] + 4) * HD]
                    nc.gpsimd.tensor_tensor(y, y, parts[:, 0:256], ALU.add)
                    pool.drain()
                    nc.gpsimd.tensor_tensor(y, y, parts[:, 256:512], ALU.add).then_inc(sm["summed"], 1)

            def attend(st, loop):
                if st[2]["who"] == "nsa":
                    attend_nsa(st, loop)
                    return
                units, _ = attention_units("stick")
                probs = bufs("stick")[0]
                for s, u in enumerate(units):
                    W = u["width"]
                    pool.wait_ge(sm["stick_scan"], value(st, "stick_scan", s + 1, loop))
                    nc.gpsimd.tensor_tensor(probs[:, s % 4, 0:W - 1], probs[:, s % 4, 0:W - 1],
                                            stick_after[:, s % 2, 1:W], ALU.mult).then_inc(sm["stick_weights"], 1)

            def mix(st, loop):
                for t in range(8):
                    pool.wait_ge(sm["parts"], value(st, "parts", t + 1, loop))
                    nc.gpsimd.tensor_tensor(part_a[:, t % 2, :], part_a[:, t % 2, :], part_b[:, t % 2, :],
                                            ALU.add).then_inc(sm["mixed"], 1)
                    pool.wait_ge(sm["split_hi"], value(st, "split_hi", t + 1, loop))
                    nc.gpsimd.tensor_tensor(h_lo[:, t, :], part_a[:, t % 2, :], h_hi[:, t, :].bitcast(F32),
                                            ALU.subtract).then_inc(sm["split_lo"], 1)

            def ffn(st, loop):
                t = 0
                for p in st[1]:
                    if not p.up:
                        continue
                    for q in range(p.tiles):
                        pool.wait_ge(sm["split_hi"], value(st, "split_hi", t + 1, loop))
                        nc.gpsimd.tensor_tensor(m_lo[:, p.tile0 + q, :], hid_m[:, t % 2, :],
                                                m_hi[:, p.tile0 + q, :].bitcast(F32),
                                                ALU.subtract).then_inc(sm["split_lo"], 1)
                        t += 1

            def stage(st, loop):
                f = dict(proj=proj, attend=attend, mix=mix, ffn=ffn).get(st[0])
                if f and not (st[0] == "attend" and st[2]["who"] in ("dil", "diff")) and not (st[0] == "proj" and st[2]["who"] == "stick"):
                    f(st, loop)
                    pool.drain().then_inc(stage_end, 1)
                else:
                    pool.sem_inc(stage_end, 1)
                pool.wait_ge(sm["stage_end"], value(st, "stage_end", 4, loop))

            pool.dma_start(mask_f[:, :], A["masks"]).then_inc(more_in, 16)
            for n, g in enumerate(("q_norm_a", "k_norm_cmp", "k_norm_slc", "k_norm_win", "q_norm_b", "k_norm_b")):
                pool.dma_start(gains[:, n, :], A[g].to_broadcast([P, HD])).then_inc(more_in, 16)
            pool.dma_start(gcol[:, 1, :], A["norm2_g"][0].rearrange("(k p) -> p k", p=P),
                           allow_slow_non_contiguous=True).then_inc(more_in, 16)
            for n, g in enumerate(("cmp_k_pos", "cmp_v_pos")):
                pool.dma_start(pos_col[:, n, :],
                               A[g][0].rearrange("(k l) d -> (l d) k", l=2),
                               allow_slow_non_contiguous=True).then_inc(more_in, 16)
            for n, g in enumerate(("cmp_k_w2", "cmp_v_w2")):
                pool.dma_start(w2_sb[:, n, :, :],
                               A[g][0].rearrange("(k p) n -> p k n", p=P)).then_inc(more_in, 16)
            for st in first:
                stage(st, None)
            with pool.Fori(0, LAYERS) as loop:
                pool.dma_start(gcol[:, 2, :], A["norm_attn_2"][bass.ds(loop, 1)].rearrange("a (k p) -> p (a k)", p=P),
                               allow_slow_non_contiguous=True).then_inc(gain_in, 16)
                for dst, src in ((gcol[:, 3, :], "norm_ffn_2"), (bgate[:, :], "b_gate_2"),
                                 (sub_col[:, 0:1], "diff_subln_2")):
                    pool.dma_start(dst, A[src][bass.ds(loop, 1)].rearrange("a (k p) -> p (a k)", p=P),
                                   allow_slow_non_contiguous=True).then_inc(col_in, 16)
                pool.dma_start(lam_init[:, :],
                               A["lam_inits"][bass.ds(loop, 1)].to_broadcast([P, 2])).then_inc(col_in, 16)
                pool.dma_start(lam_in[:, :],
                               A["diff_lambda_2"][bass.ds(loop, 1)].rearrange("a r d -> a (r d)").to_broadcast(
                                   [P, 4 * HD])).then_inc(col_in, 16)
                for st in layer:
                    stage(st, loop)
            pool.dma_start(g_final[:, :], A["norm_final_2"].unsqueeze(0).to_broadcast([P, D])).then_inc(final_in, 16)

        @block.vector
        def _(dve):
            spl = Splitter(dve, "lo")

            def turn(st, loop, hi, lo, tiles, tile0, gain):
                for t in range(tiles):
                    dve.wait_ge(sm["split_hi"], value(st, "split_hi", t + 1, loop))
                    nc.vector.scalar_tensor_tensor(lo[:, tile0 + t, :], ps[t % 8][:, :],
                                                   1.0 if gain is None else gain(t),
                                                   hi[:, tile0 + t, :].bitcast(F32), ALU.mult,
                                                   ALU.subtract).then_inc(sm["split_lo"], 1)

            def norm(st, loop):
                for i in range(QT):
                    a, b, c = (small[:, o + i:o + i + 1] for o in (0, 4, 8))
                    dve.wait_ge(sm["squares"], value(st, "squares", i + 1, loop))
                    nc.vector.tensor_scalar(b, a, 1.0 / D, EPS, ALU.mult, ALU.add).then_inc(sm["mean"], 1)
                    dve.wait_ge(sm["root"], value(st, "root", i + 1, loop))
                    nc.vector.reciprocal(c, b)
                    if st is first[0] and i == 0:
                        dve.wait_ge(consts_in, CONST_LOADS * 16)
                    dve.drain()
                    nc.vector.tensor_scalar(root_diag[:, i, :], ident, c, None, ALU.mult).then_inc(sm["scaled"], 1)
                if st is first[0] or st is layer[0]:
                    spl.upto(st, spl.next + 1, loop)
                if st is layer[0]:
                    dve.wait_ge(gain_in, loop * 16 + 16)

            def proj(st, loop):
                stage_s, stage_t, stage_u = staging(st)
                n_root, n_rope, staged, tiles, now, prev = 0, 0, 0, 0, None, None
                if st is first[1]:
                    dve.wait_ge(more_in, MORE_LOADS * 16)
                    nc.vector.tensor_copy(ident_b[:, :], ident)
                    nc.vector.tensor_copy(masks[:, :], mask_f[:, :])
                    dve.drain()
                    nc.vector.memset(cmp_in[:, :, S - 1:CMP_COLS], 0.0)
                    dve.drain()
                    for kv in range(2):
                        nc.vector.tensor_copy(cmp_in[:, 3 * kv, S:CMP_COLS:2], pos_col[:, kv, :])
                    nc.vector.memset(kc_T[:, :, :, :], 0.0)
                    nc.vector.memset(vc[:, :, :, :], 0.0)
                for k, p in enumerate(st[1]):
                    spl.upto(st, last_block(p) + SPLIT_RING, loop)
                    staged += QT
                    if p.rope is None:
                        if p.turn:
                            tiles += turn_tiles(p)
                        continue
                    nh = p.width // HD
                    full = [P, QT, nh, HD]
                    s4 = stage_s[:, :, 0:p.width].rearrange("p i (h d) -> p i h d", d=HD)
                    t4 = stage_t[:, :, 0:p.width].rearrange("p i (h d) -> p i h d", d=HD)
                    r = small[:, 64:64 + QT * nh]
                    if p.rope != now:
                        cos = tables[:, C_COS:C_COS + QT * HD].rearrange("p (i d) -> p i d", i=QT)
                        sin = tables[:, C_SIN:C_SIN + QT * HD].rearrange("p (i d) -> p i d", i=QT)
                        if p.rope >= 0:
                            g = gains[:, p.rope, :]
                            nc.vector.tensor_tensor(gcos[:, :, :], cos,
                                                    g.unsqueeze(1).to_broadcast([P, QT, HD]), ALU.mult)
                            nc.vector.tensor_tensor(gsin[:, :, 0:HALF], sin[:, :, 0:HALF],
                                                    g[:, HALF:HD].unsqueeze(1).to_broadcast([P, QT, HALF]), ALU.mult)
                            nc.vector.tensor_tensor(gsin[:, :, HALF:HD], sin[:, :, HALF:HD],
                                                    g[:, 0:HALF].unsqueeze(1).to_broadcast([P, QT, HALF]), ALU.mult)
                        else:
                            nc.vector.tensor_copy(gcos[:, :, :], cos)
                            nc.vector.tensor_copy(gsin[:, :, :], sin)
                        now = p.rope
                        dve.drain()
                    if p.rope >= 0:
                        n_root += 1
                        dve.wait_ge(sm["squares"], value(st, "squares", n_root, loop))
                        nc.vector.tensor_reduce(small[:, 128:128 + QT * nh], t4, AX_X, ALU.add)
                        dve.drain()
                        a, b = (1.0, HD * EPS) if p.query else (1.0 / HD, EPS)
                        nc.vector.tensor_scalar(small[:, 0:QT * nh], small[:, 128:128 + QT * nh], a, b, ALU.mult,
                                                ALU.add).then_inc(sm["mean"], 1)
                        dve.wait_ge(sm["root"], value(st, "root", n_root, loop))
                        nc.vector.reciprocal(r, small[:, 32:32 + QT * nh])
                        dve.drain()
                        nc.vector.tensor_tensor(s4, s4, r.rearrange("p (i h) -> p i h", i=QT).unsqueeze(3)
                                                .to_broadcast(full), ALU.mult).then_inc(sm["scaled"], 1)
                        dve.drain()
                    else:
                        dve.wait_ge(sm["staged"], value(st, "staged", staged, loop))
                        dve.sem_inc(sm["scaled"], 1)
                    n_rope += 1
                    dve.wait_ge(sm["crossed"], value(st, "crossed", n_rope, loop))
                    nc.vector.tensor_tensor(s4, s4, gcos[:, :, :].unsqueeze(2).to_broadcast(full), ALU.mult)
                    dve.drain()
                    if prev is not None:
                        dve.wait_ge(sm["turned_ps"], value(st, "turned_ps", tiles, loop))
                    if p.twice:
                        for i in range(QT):
                            pair = stage_u[:, i, 0:2 * p.width].rearrange("p (h c d) -> p h c d", c=2, d=HD)
                            nc.vector.tensor_tensor(pair[:, :, 0, :], s4[:, i, :, :], t4[:, i, :, :], ALU.add)
                            ins = nc.vector.tensor_tensor(pair[:, :, 1, :], s4[:, i, :, :], t4[:, i, :, :], ALU.add)
                        ins.then_inc(sm["roped"], 1)
                    else:
                        nc.vector.tensor_tensor(stage_u[:, :, 0:p.width], stage_s[:, :, 0:p.width],
                                                stage_t[:, :, 0:p.width], ALU.add).then_inc(sm["roped"], 1)
                    prev = p
                    tiles += turn_tiles(p)

            def compress(st, loop):
                def gelu(kv):
                    dve.wait_ge(sm["hidden_ps"], value(st, "hidden_ps", kv + 1, loop))
                    nc.vector.tensor_copy(hid_z[:, :], ps[2 + kv][:, 0:192])
                    dve.drain()
                    nc.vector.tensor_tensor(hid_s[:, :], hid_z[:, :], hid_z[:, :], ALU.mult)
                    dve.drain()
                    nc.vector.tensor_scalar(hid_s[:, :], hid_s[:, :], GELU_A * GELU_B, GELU_B, ALU.mult, ALU.add)
                    dve.drain()
                    nc.vector.tensor_tensor(hid_s[:, :], hid_s[:, :], hid_z[:, :],
                                            ALU.mult).then_inc(sm["gate_arg"], 1)
                    dve.wait_ge(sm["gate_sig"], value(st, "gate_sig", kv + 1, loop))
                    nc.vector.tensor_tensor(hid_h[:, kv, :], hid_s[:, :], hid_z[:, :],
                                            ALU.mult).then_inc(sm["hidden"], 1)

                gelu(0)
                dve.wait_ge(sm["cmp_ps"], value(st, "cmp_ps", 1, loop))
                n = slice(0, 96)
                nc.vector.tensor_copy(kc_n[n, :], ps[4][n, 0:HD])
                dve.drain()
                nc.vector.tensor_tensor(kc_t[n, :], kc_n[n, :], kc_n[n, :], ALU.mult)
                dve.drain()
                nc.vector.tensor_reduce(small[n, 0:1], kc_t[n, :], AX_X, ALU.add)
                dve.drain()
                nc.vector.tensor_scalar(small[n, 1:2], small[n, 0:1], 1.0 / HD, EPS, ALU.mult,
                                        ALU.add).then_inc(sm["mean"], 1)
                dve.wait_ge(sm["root"], value(st, "root", 1, loop))
                nc.vector.reciprocal(small[n, 2:3], small[n, 1:2])
                dve.drain()
                nc.vector.scalar_tensor_tensor(kc_n[n, :], kc_n[n, :], small[n, 2:3], gains[n, G_KC, :], ALU.mult,
                                               ALU.mult)
                dve.drain()
                nc.vector.tensor_tensor(kc_t[n, 0:HALF], kc_n[n, HALF:HD], tables[n, C_SINC:C_SINC + HALF], ALU.mult)
                nc.vector.tensor_tensor(kc_t[n, HALF:HD], kc_n[n, 0:HALF], tables[n, C_SINC + HALF:C_SINC + HD],
                                        ALU.mult)
                dve.drain()
                nc.vector.tensor_tensor(kc_n[n, :], kc_n[n, :], tables[n, C_COSC:C_COSC + HD], ALU.mult)
                dve.drain()
                nc.vector.tensor_tensor(kc_u[n, 0:HD], kc_n[n, :], kc_t[n, :], ALU.add)
                nc.vector.tensor_tensor(kc_u[n, HD:P], kc_n[n, :], kc_t[n, :], ALU.add).then_inc(sm["roped"], 1)
                gelu(1)
                shut = g_nsa[:, 0, :].rearrange("p (h b) -> p h b", b=3)[:, :, 0]
                nc.vector.tensor_scalar(shut, shut, tables[:, C_VALID:C_VALID + 1], None, ALU.mult)

            def combine(st, loop, who, u, half):
                o, i, h0, n = u["set"], u["i"], u["head0"], u["size"]
                probs, pT, parts = bufs(who)
                bank, den, nm = ps[6 + o % 2], den_t[:, u["place"], :], negmax_t[:, u["place"], :]
                if u["cmp"]:
                    den = small[:, 64 + u["h"]:64 + u["h"] + CMP_HEADS]
                w = small[:, 16:24]
                if who == "dil" and half == 0:
                    dve.drain()
                    nc.vector.tensor_reduce(small[:, 8:10], nm[:, 0:6].rearrange("p (g h) -> p h g", g=3), AX_X,
                                            ALU.min)
                    dve.drain()
                    nc.vector.tensor_tensor(small[:, 0:6].rearrange("p (g h) -> p g h", g=3),
                                            small[:, 8:10].unsqueeze(1).to_broadcast([P, 3, 2]),
                                            nm[:, 0:6].rearrange("p (g h) -> p g h", g=3),
                                            ALU.subtract).then_inc(sm["lse_gap"], 1)
                    return
                dve.wait_ge(sm["outs"], value(st, "outs", u["at"] + 1, loop))
                if who == "stick":
                    nc.vector.tensor_copy(y_two[:, i, :], bank[:, :]).then_inc(sm["combined"], 1)
                    return
                if who == "nsa":
                    gate = g_nsa[:, i, :].rearrange("p (h b) -> p b h", b=3)
                    nc.vector.reciprocal(small[:, 8:8 + n], den[:, 0:n])
                    dve.drain()
                    if u["cmp"]:
                        nc.vector.tensor_tensor(w[:, 0:n], small[:, 8:8 + n], gate[:, 0, h0:h0 + n], ALU.mult)
                        dve.drain()
                        nc.vector.tensor_tensor(y_nsa[:, i, h0 * HD:(h0 + n) * HD].rearrange("p (n d) -> p n d", n=n),
                                                bank[:, 0:n * HD].rearrange("p (n d) -> p n d", n=n),
                                                w[:, 0:n].unsqueeze(2).to_broadcast([P, n, HD]),
                                                ALU.mult).then_inc(sm["combined"], 1)
                        return
                    nc.vector.tensor_tensor(w.rearrange("p (b h) -> p b h", b=2),
                                            small[:, 8:16].rearrange("p (b h) -> p b h", b=2),
                                            gate[:, 1:3, h0:h0 + 4], ALU.mult)
                    if u["before_set"]:
                        dve.wait_ge(sm["summed"], value(st, "summed", u["before_set"], loop))
                if who == "dil":
                    dve.wait_ge(sm["lse_exp"], value(st, "lse_exp", o + 1, loop))
                    nc.vector.tensor_tensor(small[:, 24:30], small[:, 0:6], den[:, 0:6], ALU.mult)
                    dve.drain()
                    nc.vector.tensor_reduce(small[:, 30:32], small[:, 24:30].rearrange("p (g h) -> p h g", g=3), AX_X,
                                            ALU.add)
                    dve.drain()
                    nc.vector.reciprocal(small[:, 32:34], small[:, 30:32])
                    dve.drain()
                    nc.vector.tensor_tensor(w[:, 0:6].rearrange("p (g h) -> p g h", g=3),
                                            small[:, 0:6].rearrange("p (g h) -> p g h", g=3),
                                            small[:, 32:34].unsqueeze(1).to_broadcast([P, 3, 2]), ALU.mult)
                if who == "diff":
                    nc.vector.reciprocal(w[:, 0:4], den[:, 0:4])
                    dve.drain()
                    odd = w[:, 1:4:2]
                    nc.vector.tensor_scalar(odd, odd, sub_col[:, 2:3], None, ALU.mult)
                dve.drain()
                cols = n * u["vd"]
                nc.vector.tensor_tensor(parts[:, 0:cols].rearrange("p (n d) -> p n d", n=n),
                                        bank[:, 0:cols].rearrange("p (n d) -> p n d", n=n),
                                        w[:, 0:n].unsqueeze(2).to_broadcast([P, n, u["vd"]]),
                                        ALU.mult).then_inc(sm["combined"], 1)
                dve.drain()
                if who == "diff":
                    pr = parts[:, 0:512].rearrange("p (h c d) -> p h c d", h=2, c=2)
                    nc.vector.tensor_tensor(y_two[:, i, h0 * P:(h0 + 2) * P].rearrange("p (h d) -> p h d", h=2),
                                            pr[:, :, 0, :], pr[:, :, 1, :], ALU.add)
                    return
                if who == "nsa":
                    return
                y = y_dil[:, i, h0 * HD:(h0 + 2) * HD]
                nc.vector.tensor_tensor(y, parts[:, 0:128], parts[:, 128:256], ALU.add)
                dve.drain()
                nc.vector.tensor_tensor(y, y, parts[:, 256:384], ALU.add)

            def attend(st, loop):
                who = st[2]["who"]
                lag_turn, lag_out = LAGS[who]
                units, sets = attention_units(who)
                pT = bufs(who)[1]
                for s, u in enumerate(units):
                    u["at"] = s
                if who == "diff":
                    dve.wait_ge(col_in, loop * (16 * LAYER_LOADS) + 16 * LAYER_LOADS)
                    lam = lam_in[:, :].rearrange("p (a b d) -> p a b d", a=2, b=2)
                    prod = bufs(who)[2][:, 0:2 * HD].rearrange("p (a d) -> p a d", a=2)
                    nc.vector.tensor_tensor(prod, lam[:, :, 0, :], lam[:, :, 1, :], ALU.mult)
                    dve.drain()
                    nc.vector.tensor_reduce(small[:, 0:2], prod, AX_X, ALU.add).then_inc(sm["lam_dots"], 1)
                    dve.wait_ge(sm["lam_exps"], value(st, "lam_exps", 1, loop))
                    nc.vector.tensor_tensor(sub_col[:, 3:4], small[:, 3:4], small[:, 2:3], ALU.subtract)
                    dve.drain()
                    nc.vector.tensor_tensor(sub_col[:, 2:3], sub_col[:, 3:4], lam_init[:, 0:1], ALU.subtract)
                    nc.vector.tensor_tensor(sub_col[:, 1:2], sub_col[:, 0:1], lam_init[:, 1:2], ALU.mult)
                    dve.drain()
                for s in range(len(units) + lag_out + 1):
                    if s < len(units):
                        u = units[s]
                        W, o = u["width"], u["set"]
                        if who == "stick":
                            dve.wait_ge(sm["probs"], value(st, "probs", s + 1, loop))
                            if s >= 2:
                                dve.wait_ge(sm["stick_weights"], value(st, "stick_weights", s - 1, loop))
                            rem = stick_rem[:, s % 2, 0:W][:, ::-1]
                            nc.vector.tensor_tensor_scan(stick_after[:, s % 2, 0:W][:, ::-1], rem, rem, 1.0,
                                                         ALU.mult, ALU.min).then_inc(sm["stick_scan"], 1)
                        elif u["cmp"]:
                            dve.wait_ge(sm["scores"], value(st, "scores", s + 1, loop))
                            maps = ps[s % 4][:, 0:W].rearrange("p (h c) -> p h c", c=CMP_PAD)
                            g = u["h"] // CMP_HEADS
                            nm = small[:, 80 + CMP_HEADS * g:80 + CMP_HEADS * (g + 1)]
                            nc.vector.tensor_reduce(nm, maps, AX_X, ALU.max, negate=True)
                            dve.drain()
                            nc.vector.tensor_tensor(cmp_x[:, g, :].rearrange("p (h c) -> p h c", c=CMP_PAD), maps,
                                                    nm.unsqueeze(2).to_broadcast([P, CMP_HEADS, CMP_PAD]),
                                                    ALU.add).then_inc(sm["negmax"], 1)
                        else:
                            dve.wait_ge(sm["scores"], value(st, "scores", s + 1, loop))
                            nc.vector.tensor_reduce(negmax_t[:, u["place"], u["slot"]:u["slot"] + 1], ps[s % 4][:, 0:W],
                                                    AX_X, ALU.max, negate=True).then_inc(sm["negmax"], 1)
                    if 1 <= s <= len(units) and units[s - 1]["cmp"]:
                        u = units[s - 1]
                        dve.wait_ge(sm["probs"], value(st, "probs", s, loop))
                        nc.vector.tensor_reduce(small[:, 64 + u["h"]:64 + u["h"] + CMP_HEADS],
                                                bufs(who)[0][:, (s - 1) % 4, 0:u["width"]].rearrange(
                                                    "p (h c) -> p h c", c=CMP_PAD), AX_X,
                                                ALU.add).then_inc(sm["cmp_den"], 1)
                    t = s - lag_turn
                    if 0 <= t < len(units) and t % 2 == 1:
                        evac(dve, st, loop, units, t, pT, nc.vector.tensor_copy, (), "pT_dve")
                    if who == "dil" and 0 <= s - 1 < len(units) and units[s - 1]["ends_set"]:
                        combine(st, loop, who, units[s - 1], 0)
                    c = s - lag_out - 1
                    if 0 <= c < len(units) and units[c]["ends_set"]:
                        combine(st, loop, who, units[c], 1)

            def subln(st, loop):
                sq = bufs("diff")[0][:, :, :].rearrange("p a b -> p (a b)")
                y = y_two[:, :, :].rearrange("p i n -> p (i n)")
                nc.vector.tensor_tensor(sq, y, y, ALU.mult)
                dve.drain()
                nc.vector.tensor_reduce(small[:, 0:16], sq.rearrange("p (n d) -> p n d", d=P), AX_X, ALU.add)
                dve.drain()
                nc.vector.tensor_scalar(small[:, 16:32], small[:, 0:16], 1.0 / P, EPS, ALU.mult,
                                        ALU.add).then_inc(sm["mean"], 1)
                dve.wait_ge(sm["root"], value(st, "root", 1, loop))
                nc.vector.reciprocal(small[:, 32:48], small[:, 16:32])
                dve.drain()
                y3 = y.rearrange("p (n d) -> p n d", d=P)
                nc.vector.tensor_tensor(y3, y3, small[:, 32:48].unsqueeze(2).to_broadcast([P, 16, P]),
                                        ALU.mult).then_inc(sm["roped"], 1)

            def gates(st, loop):
                for p in st[1]:
                    spl.upto(st, last_block(p) + SPLIT_RING, loop)

            def mix(st, loop):
                for k, p in enumerate(st[1]):
                    spl.upto(st, last_block(p) + SPLIT_RING, loop)
                    dve.wait_ge(products, bank_count(p, 3, loop))
                    for q in range(2):
                        t = 2 * k + q
                        if t >= 2:
                            dve.wait_ge(sm["split_lo"], value(st, "split_lo", t - 1, loop))
                        nc.vector.tensor_tensor(part_a[:, t % 2, :], ps[bank_set(k) + q][:, :], gate_T[:, t, :],
                                                ALU.mult)
                        nc.vector.tensor_tensor(part_b[:, t % 2, :], ps[bank_set(k) + 2 + q][:, :],
                                                gate_T[:, 8 + t, :], ALU.mult).then_inc(sm["parts"], 1)

            def add_panel(st, k, p, loop):
                for i in range(QT):
                    dve.wait_ge(products, bank_count(p, i, loop))
                    xs = x_sb[:, i, p.col:p.col + BANK]
                    nc.vector.tensor_tensor(xs, xs, ps[bank_set(k) + i][:, :], ALU.add).then_inc(sm["added"], 1)

            def add(st, loop):
                for k, p in enumerate(st[1]):
                    spl.upto(st, last_block(p) + SPLIT_RING, loop)
                    add_panel(st, k, p, loop)

            def ffn(st, loop):
                gated = st[2]["gated"]
                m = 0
                for k, p in enumerate(st[1]):
                    spl.upto(st, last_block(p) + SPLIT_RING, loop)
                    if not p.up:
                        add_panel(st, k, p, loop)
                        continue
                    if gated:
                        dve.wait_ge(products, bank_count(p, 3, loop))
                    for q in range(p.tiles):
                        t = m + q
                        if t >= 2:
                            dve.wait_ge(sm["split_lo"], value(st, "split_lo", t - 1, loop))
                        dve.wait_ge(sm["acted"], value(st, "acted", t + 1, loop))
                        a, b = act_out[:, t % 2, :], ps[bank_set(k) + q][:, :]
                        if gated:
                            nc.vector.tensor_tensor(hid_m[:, t % 2, :], b, a, ALU.mult)
                            dve.drain()
                            nc.vector.tensor_tensor(hid_m[:, t % 2, :], ps[bank_set(k) + 2 + q][:, :],
                                                    hid_m[:, t % 2, :], ALU.mult).then_inc(sm["mixed"], 1)
                        else:
                            nc.vector.scalar_tensor_tensor(hid_m[:, t % 2, :], b, 0.0, a, ALU.max,
                                                           ALU.mult).then_inc(sm["mixed"], 1)
                    m += p.tiles

            def stage(st, loop):
                kind = st[0]
                if kind == "norm":
                    norm(st, loop)
                    turn(st, loop, h_hi, h_lo, KT, 0, lambda t: gain_col(st)[:, t:t + 1])
                elif kind == "turn":
                    turn(st, loop, m_hi, m_lo, st[2]["tiles"], st[2]["tile0"], turn_gain(st))
                else:
                    dict(proj=proj, compress=compress, attend=attend, subln=subln, gates=gates, mix=mix, add=add,
                         ffn=ffn)[kind](st, loop)
                dve.drain().then_inc(stage_end, 1)
                spl.upto(st, st[2]["spl_ahead"], loop)
                if kind not in ("add", "ffn"):
                    dve.wait_ge(sm["stage_end"], value(st, "stage_end", 4, loop))

            for st in first:
                stage(st, None)
            with dve.Fori(0, LAYERS) as loop:
                for st in layer:
                    stage(st, loop)
            for i in range(QT):
                a, b, c = (small[:, o + i:o + i + 1] for o in (0, 4, 8))
                dve.wait_ge(sm["squares"], total["squares"] + per_layer["squares"] + i + 1)
                nc.vector.tensor_scalar(b, a, 1.0 / D, EPS, ALU.mult, ALU.add).then_inc(sm["mean"], 1)
                dve.wait_ge(sm["root"], total["root"] + per_layer["root"] + i + 1)
                nc.vector.reciprocal(c, b)
                if i == 0:
                    dve.wait_ge(final_in, 16)
                dve.drain()
                nc.vector.scalar_tensor_tensor(out_sb[:, i, :], x_sb[:, i, :], c, g_final[:, :],
                                               ALU.mult, ALU.mult).then_inc(sm["out_ready"], 1)

        @block.tensor
        def _(pe):
            def turn(st, loop, src, tiles):
                for t in range(tiles):
                    if t >= 8:
                        pe.wait_ge(sm["split_lo"], value(st, "split_lo", t - 7, loop))
                    for i in range(QT):
                        ins = nc.tensor.transpose(ps[t % 8][:, i * P:(i + 1) * P], src[:, i, t * P:(t + 1) * P], ident)
                    ins.then_inc(sm["turned_ps"], 1)

            def turn_normed(st, loop):
                for i in range(QT):
                    pe.wait_ge(sm["scaled"], value(st, "scaled", i + 1, loop))
                    for t in range(KT):
                        ins = nc.tensor.matmul(ps[t][:, i * P:(i + 1) * P], x_sb[:, i, t * P:(t + 1) * P],
                                               root_diag[:, i, :], start=True, stop=True)
                        if i == QT - 1:
                            ins.then_inc(sm["turned_ps"], 1)

            def multiply(p, b, k_at, base, x_hi, x_lo, natural, loop):
                slot = b.spl % SPLIT_RING
                hi, lo = view(w_hi, slot, b), view(w_lo, slot, b)
                for q in range(QT):
                    for k in range(b.kts):
                        kt = k_at + k
                        n = slice(q * P, (q + 1) * P)
                        if natural:
                            o = ps[base + q][:, 0:b.width]
                            ops = ((x_hi[:, kt, n], hi[:, k, :]), (x_hi[:, kt, n], lo[:, k, :]),
                                   (x_lo[:, kt, n], hi[:, k, :]))
                        else:
                            o = ps[base + q][:, :]
                            ops = ((hi[:, k, n], x_hi[:, kt, :]), (hi[:, k, n], x_lo[:, kt, :]),
                                   (lo[:, k, n], x_hi[:, kt, :]))
                        for e, (l, r) in enumerate(ops):
                            ins = nc.tensor.matmul(o, l, r, start=(kt == 0 and e == 0),
                                                   stop=(kt == p.kts - 1 and e == 2))
                    ins.then_inc(products, 1)

            def gemm(st, p, base, x_hi, x_lo, natural, loop):
                k_at = 0
                for b in p.blocks:
                    if p is st[1][0] and st[2]["follows"] in ("norm", "mix"):
                        pe.wait_ge(sm["split_lo"], value(st, "split_lo", k_at + b.kts - KT, loop))
                        if st[2]["follows"] == "mix":
                            pe.wait_ge(sm["parts"], value(st, "parts", -2, loop))
                    if st[0] == "ffn" and not p.up:
                        pe.wait_ge(sm["split_lo"], value(st, "split_lo", p.tiles_before + k_at + b.kts, loop))
                    pe.wait_ge(w_lo_ready, of_blocks(b.spl + 1, 1, loop))
                    multiply(p, b, k_at, base, x_hi, x_lo, natural, loop)
                    k_at += b.kts

            def proj(st, loop):
                stage_s, stage_t, stage_u = staging(st)
                tiles, staged, ropes, pending = 0, 0, 0, None
                released = {}

                def turn_panel(p):
                    nonlocal tiles
                    if p.rope is not None:
                        pe.wait_ge(sm["roped"], value(st, "roped", p.roped_at, loop))
                    else:
                        pe.wait_ge(sm["staged"], value(st, "staged", p.staged_at, loop))
                    for c in range(turn_tiles(p)):
                        if c >= 4:
                            pe.wait_ge(sm["turned"], value(st, "turned", tiles - 3, loop))
                        for i in range(QT):
                            src = stage_u[:, i, c * P:(c + 1) * P]
                            ins = nc.tensor.transpose(ps[p.set + c % 4][:, i * P:(i + 1) * P], src, ident)
                        ins.then_inc(sm["turned_ps"], 1)
                        tiles += 1
                    released[p.set] = tiles

                for k, p in enumerate(st[1]):
                    p.set = bank_set(k)
                    staged += QT
                    p.staged_at = staged
                    if p.rope is not None:
                        ropes += 1
                        p.roped_at = ropes
                    if k >= 2:
                        pe.wait_ge(sm["staged"], value(st, "staged", staged - 2 * QT, loop))
                    if released.get(p.set):
                        pe.wait_ge(sm["turned"], value(st, "turned", released[p.set], loop))
                    gemm(st, p, p.set, h_hi, h_lo, True, loop)
                    if pending is not None:
                        turn_panel(pending)
                        pending = None
                    if p.rope is not None or p.turn:
                        pending = p
                if pending is not None:
                    turn_panel(pending)

            def compress(st, loop):
                b0 = st[1][0].blocks
                tokens = cmp_in[:, :, :].rearrange("p g c -> p (g c)")

                def pre(kv, half):
                    b = b0[2 * kv + half]
                    pe.wait_ge(landed[b.raw % RAW_RING], landing(b, loop))
                    w = raw_direct(b)
                    for k in range(8):
                        kt = half * 8 + k
                        c = 3 * kv * CMP_COLS + 2 * kt
                        ins = nc.tensor.matmul(ps[kv][0:CMP_ROWS, 0:CMP_HID],
                                               tokens[:, c:c + CMP_STRIDE * (CMP_ROWS - 1) + 1:CMP_STRIDE],
                                               w[:, k, :], start=kt == 0, stop=kt == 15)
                    ins.then_inc(direct_used, 1)

                def spread(kv):
                    pe.wait_ge(sm["pre"], value(st, "pre", kv + 1, loop))
                    for ht in range(2):
                        ins = nc.tensor.matmul(ps[2 + kv][:, ht * 96:ht * 96 + 96],
                                               cmp_pre[0:CMP_ROWS, kv, ht * P:(ht + 1) * P],
                                               tables[0:CMP_ROWS, C_SPREAD:C_SPREAD + 96], start=True, stop=True)
                    ins.then_inc(sm["hidden_ps"], 1)

                pre(0, 0)
                pre(0, 1)
                pe.drain().then_inc(sm["pre_ps"], 1)
                spread(0)
                pre(1, 0)
                pe.wait_ge(sm["hidden"], value(st, "hidden", 1, loop))
                for ht in range(2):
                    ins = nc.tensor.matmul(ps[4][0:96, 0:HD], hid_h[:, 0, ht * 96:ht * 96 + 96], w2_sb[:, 0, ht, :],
                                           start=ht == 0, stop=ht == 1)
                ins.then_inc(sm["cmp_ps"], 1)
                pre(1, 1)
                pe.drain().then_inc(sm["pre_ps"], 1)
                spread(1)
                pe.wait_ge(sm["roped"], value(st, "roped", 1, loop))
                nc.tensor.transpose(ps[6][:, 0:96], kc_u[0:96, :],
                                    ident[0:96, 0:96]).then_inc(sm["turned_ps"], 1)
                pe.wait_ge(sm["hidden"], value(st, "hidden", 2, loop))
                for copy in range(CMP_HEADS):
                    for g in range(3):
                        for ht in range(2):
                            ins = nc.tensor.matmul(ps[5][copy * CMP_PAD:(copy + 1) * CMP_PAD, g * HD:(g + 1) * HD],
                                                   hid_h[:, 1, ht * 96 + g * 32:ht * 96 + g * 32 + 32],
                                                   w2_sb[:, 1, ht, :], start=ht == 0, stop=ht == 1)
                ins.then_inc(sm["cmp_ps"], 1)

            def operands(who, u):
                i, h, br = u["i"], u["h"], u["br"]
                r = slice(HD * (h % 2), HD * (h % 2) + HD)
                n, kn = slice(i * P, (i + 1) * P), slice(u["j0"] * P, (i + 1) * P)
                if who == "nsa":
                    g = h // (NSA_HEADS // NSA_GROUPS)
                    q = dest["qa"][r, h // 2, n]
                    k = dest["ks" if br == 0 else "kw"][r, g, kn]
                    c = 192 * br + g * HD
                    return q, k, lambda j: v_nsa[:, j, c:c + HD]
                if who == "dil":
                    return (dest["qb"][r, h // 2, n], dest["kb"][r, h // 2, kn],
                            lambda j: v_dil[:, j, h * HD:(h + 1) * HD])
                c = (h // 2) * P if who == "diff" else h * HD
                return dest["dq"][r, h // 2, n], dest["dk"][r, h // 2, kn], lambda j: v_two[:, j, c:c + u["vd"]]

            def attend(st, loop):
                who = st[2]["who"]
                lag_turn, lag_out = LAGS[who]
                units, sets = attention_units(who)
                probs, pT, _ = bufs(who)
                for s in range(len(units) + lag_out):
                    if s < len(units):
                        u = units[s]
                        pair = (s, s + 1) if u["slot"] % 2 == 0 and not u["cmp"] else (s,) if u["cmp"] else ()
                        if pair and pair[-1] >= 4:
                            pe.wait_ge(sm["probs"], value(st, "probs", pair[-1] - 3, loop))
                        if u["cmp"]:
                            m0 = N_MASK * P + u["i"] * CMP_PAD
                            nc.tensor.matmul(ps[s % 4][:, 0:u["width"]].rearrange("p (h c) -> p h c", c=CMP_PAD),
                                             ident_b[:, :], masks[:, m0:m0 + CMP_PAD].unsqueeze(1).to_broadcast(
                                                 [P, CMP_HEADS, CMP_PAD]), start=True, stop=False)
                            for n in range(CMP_HEADS // 2):
                                ins = nc.tensor.matmul(ps[s % 4][:, 2 * n * CMP_PAD:2 * (n + 1) * CMP_PAD],
                                                       dest["qa"][:, u["h"] // 2 + n, u["i"] * P:(u["i"] + 1) * P],
                                                       kc_T[:, u["h"] // CMP_HEADS, :, :].rearrange("p a c -> p (a c)"),
                                                       start=False, stop=n == CMP_HEADS // 2 - 1)
                            ins.then_inc(sm["scores"], 1)
                        elif pair:
                            for r in pair:
                                q, k, _v = operands(who, units[r])
                                nc.tensor.matmul(ps[r % 4][:, 0:u["width"]], q, k, start=True, stop=False)
                            for r in pair:
                                for n, (c, m) in enumerate(u["masks"]):
                                    ins = nc.tensor.matmul(ps[r % 4][:, c:c + P], ident_b[:, :],
                                                           masks[:, m * P:(m + 1) * P],
                                                           start=False, stop=n == len(u["masks"]) - 1)
                                ins.then_inc(sm["scores"], 1)
                    t = s - lag_turn
                    if 0 <= t < len(units):
                        u = units[t]
                        if who == "stick":
                            pe.wait_ge(sm["stick_weights"], value(st, "stick_weights", t + 1, loop))
                        else:
                            pe.wait_ge(sm["probs"], value(st, "probs", t + 1, loop))
                        if t >= 2:
                            if t % 2:
                                pe.wait_ge(sm["pT_dve"], value(st, "pT_dve", t // 2, loop))
                            else:
                                pe.wait_ge(sm["pT_act"], value(st, "pT_act", t // 2, loop))
                        for j in range(u["nj"]):
                            ins = nc.tensor.transpose(ps[4 + t % 2][:, j * P:(j + 1) * P],
                                                      probs[:, t % 4, j * P:(j + 1) * P], ident)
                        ins.then_inc(sm["probs_turned"], 1)
                    v = s - lag_out
                    if 0 <= v < len(units):
                        u = units[v]
                        if u["cmp"]:
                            pe.wait_ge(sm["cmp_den"], value(st, "cmp_den", u["i"] * 3 + u["h"] // CMP_HEADS + 1, loop))
                        if v % 2:
                            pe.wait_ge(sm["pT_dve"], value(st, "pT_dve", v // 2 + 1, loop))
                        else:
                            pe.wait_ge(sm["pT_act"], value(st, "pT_act", v // 2 + 1, loop))
                        if u["slot"] == 0 and u["set"] >= 2:
                            pe.wait_ge(sm["combined"], value(st, "combined", u["set"] - 1, loop))
                        if u["cmp"]:
                            ins = nc.tensor.matmul(ps[6 + u["set"] % 2][:, 0:CMP_HEADS * HD], pT[v % 4][:, 0:P],
                                                   vc[:, u["h"] // CMP_HEADS, :, :].rearrange("p h d -> p (h d)"),
                                                   start=True, stop=True)
                        else:
                            values = operands(who, u)[2]
                            o = ps[6 + u["set"] % 2][:, u["slot"] * u["vd"]:(u["slot"] + 1) * u["vd"]]
                            for j in range(u["nj"]):
                                ins = nc.tensor.matmul(o, pT[v % 4][:, j * P:(j + 1) * P], values(u["j0"] + j),
                                                       start=j == 0, stop=j == u["nj"] - 1)
                        ins.then_inc(sm["outs"], 1)

            def gates(st, loop):
                for k, p in enumerate(st[1]):
                    if k >= 2:
                        pe.wait_ge(sm["gated"], value(st, "gated", 4 * (k - 1), loop))
                    gemm(st, p, bank_set(k), h_hi, h_lo, False, loop)

            def mix(st, loop):
                for k, p in enumerate(st[1]):
                    cut, k_at, base = p.split_at, 0, bank_set(k)
                    if k >= 2:
                        pe.wait_ge(sm["parts"], value(st, "parts", 2 * (k - 1), loop))
                    for b in p.blocks:
                        pe.wait_ge(w_lo_ready, of_blocks(b.spl + 1, 1, loop))
                        slot = b.spl % SPLIT_RING
                        hi, lo = view(w_hi, slot, b), view(w_lo, slot, b)
                        parts = [(0, 0, cut), (2, cut, KT)]
                        parts = [(o, max(a, k_at), min(e, k_at + b.kts), a, e) for o, a, e in parts]
                        parts = [x for x in parts if x[1] < x[2]]
                        for o, ka, kb, a, e in parts:
                            for q in range(2):
                                n = slice(q * P, (q + 1) * P)
                                for kt in range(ka, kb):
                                    kk = kt - k_at
                                    ops = ((hi[:, kk, n], m_hi[:, kt, :]), (hi[:, kk, n], m_lo[:, kt, :]),
                                           (lo[:, kk, n], m_hi[:, kt, :]))
                                    for m, (l, r) in enumerate(ops):
                                        ins = nc.tensor.matmul(ps[base + o + q][:, :], l, r,
                                                               start=(kt == a and m == 0),
                                                               stop=(kt == e - 1 and m == 2))
                                ins.then_inc(products, 4 // (2 * len(parts)))
                        k_at += b.kts

            def add(st, loop):
                for k, p in enumerate(st[1]):
                    gemm(st, p, bank_set(k), h_hi, h_lo, True, loop)

            def ffn(st, loop):
                done = {"up": 0, "down": 0}
                readers = []
                for k, p in enumerate(st[1]):
                    if k >= 2:
                        pe.wait_ge(sm[readers[k - 2][0]], value(st, *readers[k - 2], loop))
                    if p.up:
                        done["up"] += p.tiles
                        readers.append(("mixed", done["up"]))
                        gemm(st, p, bank_set(k), h_hi, h_lo, False, loop)
                    else:
                        p.tiles_before = done["up"] - p.kts
                        done["down"] += QT
                        readers.append(("added", done["down"]))
                        gemm(st, p, bank_set(k), m_hi, m_lo, True, loop)

            def stage(st, loop):
                kind = st[0]
                if kind == "norm":
                    turn_normed(st, loop)
                elif kind == "turn":
                    turn(st, loop, dict(y_nsa=y_nsa, y_dil=y_dil, y_diff=y_two)[st[2]["src"]], st[2]["tiles"])
                elif kind != "subln":
                    dict(proj=proj, compress=compress, attend=attend, gates=gates, mix=mix, add=add,
                         ffn=ffn)[kind](st, loop)
                if kind == "subln":
                    pe.sem_inc(stage_end, 1)
                else:
                    pe.drain().then_inc(stage_end, 1)
                if kind not in ("norm", "mix"):
                    pe.wait_ge(sm["stage_end"], value(st, "stage_end", 4, loop))

            for st in first:
                stage(st, None)
            with pe.Fori(0, LAYERS) as loop:
                for st in layer:
                    stage(st, loop)


def shape_tables():
    import numpy as np

    half = np.arange(HALF, dtype=np.float32)
    inv = np.power(np.float32(10000.0), -half / np.float32(HALF)).astype(np.float32)

    def cos_sin(pos):
        ang = pos.astype(np.float32)[:, None] * inv[None, :]
        c, s = np.cos(ang), np.sin(ang)
        return np.concatenate([c, c], 1), np.concatenate([-s, s], 1)

    tables = np.zeros((P, C_ALL), np.float32)
    c, s = cos_sin(np.arange(S))
    tables[:, C_COS:C_COS + 256] = c.reshape(QT, P, HD).transpose(1, 0, 2).reshape(P, 256)
    tables[:, C_SIN:C_SIN + 256] = s.reshape(QT, P, HD).transpose(1, 0, 2).reshape(P, 256)
    c_end = np.arange(CMP_PAD) * CMP_STRIDE + CMP_LEN - 1
    c, s = cos_sin(c_end)
    tables[0:96, C_COSC:C_COSC + HD] = np.tile(c, (3, 1))
    tables[0:96, C_SINC:C_SINC + HD] = np.tile(s, (3, 1))
    tables[:, C_VALID] = np.arange(P) >= CMP_LEN - 1
    tables[:, C_ID:C_ID + P] = np.eye(P)
    for g in range(NSA_GROUPS):
        for c in range(CMP_PAD):
            tables[g * (CMP_COLS // CMP_STRIDE) + c, C_SPREAD + g * CMP_PAD + c] = 1.0
    tables[S // CMP_STRIDE, C_SPREAD:C_SPREAD + 96] = 1.0
    q, k = np.arange(P)[:, None], np.arange(P)[None, :]
    m4, m16, causal = (q - k) % 4 == 0, (q - k) % 16 == 0, k <= q
    seen = [causal, k >= q, m4, m4 & causal, m16, m16 & causal, k < q]
    for i in range(QT):
        c = np.arange(CMP_PAD)[None, :]
        seen.append((c < CMP_N) & (c_end[None, :] <= q + i * P))
    masks = np.concatenate([np.where(m, 0.0, NEG) for m in seen], 1).astype(np.float32)
    import math
    li = [0.8 - 0.6 * math.exp(-0.3 * n) for n in range(LAYERS)]
    lam = np.array([[v, 1.0 - v] for v in li], np.float32)
    return dict(tables=tables, masks=masks, lam_inits=lam)


_INS = ("x norm1_g w_in q_norm_a k_norm_cmp k_norm_slc k_norm_win cmp_k_pos cmp_k_w1 cmp_k_w2 cmp_v_pos cmp_v_w1 "
        "cmp_v_w2 q_norm_b k_norm_b w_o_a w_o_b w_out norm2_g w_up w_down norm_attn_2 w_in_2 b_gate_2 diff_lambda_2 "
        "diff_subln_2 w_o_diff_2 w_o_sb_2 w_out_2 norm_ffn_2 w_ffn_in_2 w_ffn_out_2 norm_final_2").split()


def kernel(**inputs):
    import numpy as _np
    import concourse.bacc as _bacc
    from concourse.bass_utils import run_bass_kernel_spmd as _run

    nc = _bacc.Bacc("TRN2", target_bir_lowering=False, num_devices=1)
    arrays = {f"in_{n}": _np.ascontiguousarray(inputs[n]) for n in _INS}
    arrays.update({f"in_{n}": a for n, a in shape_tables().items()})
    aps = {n[3:]: nc.dram_tensor(n, a.shape, F32, kind="ExternalInput").ap() for n, a in arrays.items()}
    out = nc.dram_tensor("out", (1, S, D), F32, kind="ExternalOutput").ap()
    build(nc, aps, out)
    r = _run(nc, [arrays], core_ids=[0])
    return r.results[0]["out"]
```
